# Optimizing a Trainium2 kernel written in Bass

```python
import jax
import jax.numpy as jnp
from jax import lax
import numpy as np

D_MODEL = 1024
BATCH = 1
SEQ = 256
DEPTH = 2

CHUNK = 64
PLE_DIM = 256
N_MIXERS = 2
N_LAYERS_A = (DEPTH + 1) // 2
N_LAYERS_B = DEPTH // 2
EPS = 1e-6

GMLP_BLOCK = 128
GMLP_DIM = 2 * D_MODEL
GMLP_GROUPS = 8
GMLP_GROUP_DIM = GMLP_DIM // GMLP_GROUPS

MLSTM_INNER = 2 * D_MODEL
MLSTM_HEADS = 8
MLSTM_HEAD_DIM = MLSTM_INNER // MLSTM_HEADS
MLSTM_CONV = 4
QKV_BLOCK = 4
QKV_NBLK = MLSTM_INNER // QKV_BLOCK

D_FF = 2816
N_EXPERTS = 8
TOP_K = 2

kernel_name = 'hybrid_gmlp_mlstm_moe_streaming'

def rms_norm(x, g):
    xf = x.astype(jnp.float32)
    y = xf * lax.rsqrt(jnp.mean(xf * xf, axis=-1, keepdims=True) + EPS)
    return (y * g.astype(jnp.float32)).astype(x.dtype)

def layer_norm(x, g, b):
    xf = x.astype(jnp.float32)
    xc = xf - jnp.mean(xf, axis=-1, keepdims=True)
    y = xc * lax.rsqrt(jnp.mean(xc * xc, axis=-1, keepdims=True) + EPS)
    return (y * g.astype(jnp.float32) + b.astype(jnp.float32)).astype(x.dtype)

def swiglu(h, w_gate, w_up, w_down):
    return (jax.nn.silu(h @ w_gate) * (h @ w_up)) @ w_down

def chunk_causal_mask(n):
    c = jnp.arange(n) // CHUNK
    return c[:, None] >= c[None, :]

def gmlp_mixer(h, w_in, ln_g, ln_b, w_s, b_s, w_out):
    B, S, _ = h.shape
    nb = S // GMLP_BLOCK
    uv = jax.nn.gelu(h @ w_in, approximate=False)
    u, v = jnp.split(uv, 2, axis=-1)
    v = layer_norm(v, ln_g, ln_b)
    v = v.reshape(B, nb, GMLP_BLOCK, GMLP_GROUPS, GMLP_GROUP_DIM)
    w = jnp.where(chunk_causal_mask(GMLP_BLOCK)[None], w_s, 0.0).astype(v.dtype)
    mixed = jnp.einsum('gts,bnsgc->bntgc', w, v) + b_s.T.astype(v.dtype)[None, None, :, :, None]
    return (u * mixed.reshape(B, S, GMLP_DIM)) @ w_out

def causal_conv(x, w, b):
    K = w.shape[0]
    S = x.shape[1]
    xp = jnp.pad(x, ((0, 0), (K - 1, 0), (0, 0)))
    out = b
    for j in range(K):
        out = out + xp[:, j:j + S] * w[j]
    return out

def block_diag_proj(x, w):
    B, S, C = x.shape
    xb = x.reshape(B, S, QKV_NBLK, QKV_BLOCK)
    return jnp.einsum('bsnc,ncd->bsnd', xb, w).reshape(B, S, C)

def mlstm_chunkwise(q, k, v, log_i, log_f):
    B, H, S, dh = q.shape
    nc = S // CHUNK
    q = q * dh ** -0.5

    def to_chunks(a):
        return jnp.moveaxis(a.reshape((B, H, nc, CHUNK) + a.shape[3:]), 2, 0)

    xs = (to_chunks(q), to_chunks(k), to_chunks(v), to_chunks(log_i), to_chunks(log_f))
    causal = jnp.tril(jnp.ones((CHUNK, CHUNK), dtype=bool))

    def step(carry, inp):
        C, n, m = carry
        qj, kj, vj, li, lf = inp
        bcum = jnp.cumsum(lf, axis=-1)
        d = bcum[..., :, None] - bcum[..., None, :] + li[..., None, :]
        d = jnp.where(causal, d, -jnp.inf)
        inter = bcum + m[..., None]
        m_t = jnp.maximum(jnp.max(d, axis=-1), inter)
        w_intra = jnp.exp(d - m_t[..., None])
        w_inter = jnp.exp(inter - m_t)
        s = jnp.einsum('bhtd,bhsd->bhts', qj, kj) * w_intra
        num = jnp.einsum('bhts,bhsd->bhtd', s, vj) + w_inter[..., None] * jnp.einsum('bhvk,bhtk->bhtv', C, qj)
        qn = jnp.sum(s, axis=-1) + w_inter * jnp.einsum('bhk,bhtk->bht', n, qj)
        h = num / jnp.maximum(jnp.abs(qn), jnp.exp(-m_t))[..., None]
        b_last = bcum[..., -1]
        m_new = m_t[..., -1]
        w_state = jnp.exp(b_last[..., None] - bcum + li - m_new[..., None])
        decay = jnp.exp(b_last + m - m_new)
        C_new = decay[..., None, None] * C + jnp.einsum('bhsv,bhsk->bhvk', vj * w_state[..., None], kj)
        n_new = decay[..., None] * n + jnp.einsum('bhs,bhsk->bhk', w_state, kj)
        return (C_new, n_new, m_new), h

    init = (jnp.zeros((B, H, dh, dh), jnp.float32), jnp.zeros((B, H, dh), jnp.float32),
            jnp.zeros((B, H), jnp.float32))
    _, hs = lax.scan(step, init, xs)
    return jnp.moveaxis(hs, 0, 2).reshape(B, H, S, dh)

def mlstm_mixer(h, w_in, conv_w, conv_b, wq, wk, wv, w_gate, b_gate, norm_g, skip, w_out):
    B, S, _ = h.shape
    H, dh = MLSTM_HEADS, MLSTM_HEAD_DIM
    xm, z = jnp.split(h @ w_in, 2, axis=-1)
    xc = jax.nn.silu(causal_conv(xm, conv_w, conv_b))
    q = block_diag_proj(xc, wq)
    k = block_diag_proj(xc, wk)
    v = block_diag_proj(xm, wv)
    gates = (jnp.concatenate([q, k, v], axis=-1) @ w_gate + b_gate).astype(jnp.float32)
    log_i = gates[..., :H].transpose(0, 2, 1)
    log_f = jax.nn.log_sigmoid(gates[..., H:]).transpose(0, 2, 1)

    def heads(a):
        return a.reshape(B, S, H, dh).transpose(0, 2, 1, 3).astype(jnp.float32)

    hc = mlstm_chunkwise(heads(q), heads(k), heads(v), log_i, log_f).transpose(0, 2, 1, 3)
    hc = hc - jnp.mean(hc, axis=-1, keepdims=True)
    hn = hc * lax.rsqrt(jnp.mean(hc * hc, axis=-1, keepdims=True) + EPS)
    hn = hn.reshape(B, S, MLSTM_INNER).astype(h.dtype) * norm_g
    out = jax.nn.sigmoid(z) * (hn + skip * xc)
    return out @ w_out

def moe_swiglu(h, router, w_gate, w_up, w_down):
    logits = (h @ router).astype(jnp.float32)
    top_v, top_i = lax.top_k(logits, TOP_K)
    probs = jax.nn.softmax(top_v, axis=-1)
    combine = jnp.sum(jax.nn.one_hot(top_i, N_EXPERTS, dtype=jnp.float32) * probs[..., None], axis=-2)
    combine = combine.astype(h.dtype)
    out = jnp.zeros_like(h)
    for e in range(N_EXPERTS):
        out = out + combine[..., e:e + 1] * swiglu(h, w_gate[e], w_up[e], w_down[e])
    return out

def setup_inputs(seed: int = 0) -> dict:
    key = jax.random.key(seed)
    ks = iter(list(jax.random.split(key, 64)))

    def nrm(shape, scale):
        return jax.random.normal(next(ks), shape, jnp.float32) * scale

    def gain(shape):
        return 1.0 + nrm(shape, 0.05)

    NA, NB, H = N_LAYERS_A, N_LAYERS_B, MLSTM_HEADS
    fgate_bias = jnp.linspace(3.0, 6.0, H, dtype=jnp.float32)
    b_gate = jnp.concatenate([nrm((NB, H), 0.1), fgate_bias[None] + nrm((NB, H), 0.1)], axis=-1)
    return {
        'x': nrm((BATCH, SEQ, D_MODEL), 1.0),
        'p': nrm((DEPTH, BATCH, SEQ, PLE_DIM), 1.0),
        'norm_mix': gain((DEPTH, D_MODEL)),
        'norm_ffn': gain((DEPTH, D_MODEL)),
        'norm_ple': gain((DEPTH, D_MODEL)),
        'norm_final': gain((D_MODEL,)),
        'ga_w_in': nrm((NA, D_MODEL, 2 * GMLP_DIM), D_MODEL ** -0.5),
        'ga_ln_g': gain((NA, GMLP_DIM)),
        'ga_ln_b': nrm((NA, GMLP_DIM), 0.02),
        'ga_w_s': nrm((NA, GMLP_GROUPS, GMLP_BLOCK, GMLP_BLOCK), GMLP_BLOCK ** -0.5),
        'ga_b_s': 1.0 + nrm((NA, GMLP_GROUPS, GMLP_BLOCK), 0.1),
        'ga_w_out': nrm((NA, GMLP_DIM, D_MODEL), GMLP_DIM ** -0.5),
        'mb_w_in': nrm((NB, D_MODEL, 2 * MLSTM_INNER), D_MODEL ** -0.5),
        'mb_conv_w': nrm((NB, MLSTM_CONV, MLSTM_INNER), MLSTM_CONV ** -0.5),
        'mb_conv_b': nrm((NB, MLSTM_INNER), 0.02),
        'mb_wq': nrm((NB, QKV_NBLK, QKV_BLOCK, QKV_BLOCK), QKV_BLOCK ** -0.5),
        'mb_wk': nrm((NB, QKV_NBLK, QKV_BLOCK, QKV_BLOCK), QKV_BLOCK ** -0.5),
        'mb_wv': nrm((NB, QKV_NBLK, QKV_BLOCK, QKV_BLOCK), QKV_BLOCK ** -0.5),
        'mb_w_gate': nrm((NB, 3 * MLSTM_INNER, 2 * H), (3 * MLSTM_INNER) ** -0.5),
        'mb_b_gate': b_gate,
        'mb_norm_g': gain((NB, MLSTM_INNER)),
        'mb_skip': gain((NB, MLSTM_INNER)),
        'mb_w_out': nrm((NB, MLSTM_INNER, D_MODEL), MLSTM_INNER ** -0.5),
        'fd_w_gate': nrm((NA, D_MODEL, D_FF), D_MODEL ** -0.5),
        'fd_w_up': nrm((NA, D_MODEL, D_FF), D_MODEL ** -0.5),
        'fd_w_down': nrm((NA, D_FF, D_MODEL), D_FF ** -0.5),
        'fe_router': nrm((NB, D_MODEL, N_EXPERTS), D_MODEL ** -0.5),
        'fe_w_gate': nrm((NB, N_EXPERTS, D_MODEL, D_FF), D_MODEL ** -0.5),
        'fe_w_up': nrm((NB, N_EXPERTS, D_MODEL, D_FF), D_MODEL ** -0.5),
        'fe_w_down': nrm((NB, N_EXPERTS, D_FF, D_MODEL), D_FF ** -0.5),
        'ple_w_proj': nrm((DEPTH, PLE_DIM, D_MODEL), PLE_DIM ** -0.5),
        'ple_w_gate': nrm((DEPTH, D_MODEL, D_MODEL), D_MODEL ** -0.5),
    }

def reference(x, p, norm_mix, norm_ffn, norm_ple, norm_final,
              ga_w_in, ga_ln_g, ga_ln_b, ga_w_s, ga_b_s, ga_w_out,
              mb_w_in, mb_conv_w, mb_conv_b, mb_wq, mb_wk, mb_wv, mb_w_gate, mb_b_gate,
              mb_norm_g, mb_skip, mb_w_out,
              fd_w_gate, fd_w_up, fd_w_down,
              fe_router, fe_w_gate, fe_w_up, fe_w_down,
              ple_w_proj, ple_w_gate):
    for i in range(DEPTH):
        j = i // 2
        h = rms_norm(x, norm_mix[i])
        if i % N_MIXERS == 0:
            x = x + gmlp_mixer(h, ga_w_in[j], ga_ln_g[j], ga_ln_b[j], ga_w_s[j], ga_b_s[j], ga_w_out[j])
        else:
            x = x + mlstm_mixer(h, mb_w_in[j], mb_conv_w[j], mb_conv_b[j], mb_wq[j], mb_wk[j], mb_wv[j],
                                mb_w_gate[j], mb_b_gate[j], mb_norm_g[j], mb_skip[j], mb_w_out[j])
        h = rms_norm(x, norm_ffn[i])
        if i % 2 == 0:
            x = x + swiglu(h, fd_w_gate[j], fd_w_up[j], fd_w_down[j])
        else:
            x = x + moe_swiglu(h, fe_router[j], fe_w_gate[j], fe_w_up[j], fe_w_down[j])
        g = jax.nn.sigmoid(rms_norm(x, norm_ple[i]) @ ple_w_gate[i])
        x = x + g * (p[i] @ ple_w_proj[i])
    return rms_norm(x, norm_final)


_drawn_inputs = setup_inputs


def setup_inputs(seed=0):
    import zlib

    import numpy as np

    out = dict(_drawn_inputs(seed))
    spreads = {}
    factors = {'norm_ple': 4.755,
     'ga_ln_b': 2.768,
     'mb_conv_b': 3.865,
     'mb_norm_g': 3.001,
     'mb_skip': 3.589}
    for name, (base, spread) in spreads.items():
        noise = np.random.default_rng([zlib.crc32(name.encode()), seed]).standard_normal(out[name].shape)
        drawn = base * np.exp(spread * noise) if base else spread * noise
        out[name] = jnp.asarray(drawn.astype(out[name].dtype))
    for name, factor in factors.items():
        out[name] = (out[name] * factor).astype(out[name].dtype)
    return out
```

```python
from contextlib import ExitStack

import concourse.bass as bass
from concourse import mybir

F32 = mybir.dt.float32
F32R = mybir.dt.float32r
I32 = mybir.dt.int32
ALU = mybir.AluOpType
ACT = mybir.ActivationFunctionType
AX = mybir.AxisListType

P = 128
EPS = 1e-6
BIG = 3.0e38
RSQRT_SEED = 1597463007.0


def stream_positions(n_blocks):
    gate_up, down, order = {}, {}, []
    for b in range(n_blocks + 2):
        if b < n_blocks:
            gate_up[b] = len(order)
            order += [("gu", b, 0), ("gu", b, 1)]
        if b >= 2:
            down[b - 2] = len(order)
            order.append(("down", b - 2, 0))
    return gate_up, down, order


def build(nc, A, out):
    _, T, D = A["x"].shape
    NT = T // P
    KD = D // P
    PLE = A["p"].shape[-1]
    KP = PLE // P
    G = A["ga_w_s"].shape[1]
    GD = A["ga_ln_g"].shape[1]
    KG = GD // P
    H = A["mb_w_gate"].shape[-1] // 2
    DI = A["mb_w_in"].shape[-1] // 2
    KI = DI // P
    DH = DI // H
    CONV = A["mb_conv_w"].shape[1]
    NBLK = A["mb_wq"].shape[1]
    QB = A["mb_wq"].shape[2]
    E = A["fe_router"].shape[-1]
    F = A["fd_w_gate"].shape[-1]
    FB = 256
    NB = F // FB
    CW = 512
    assert NT == 2 and KD == 8 and KP == 2 and KG == 16 and KI == 16 and H == G == E == 8 and DH == 256
    assert NB * FB == F and QB == 4 and NBLK == 32 * KI and CONV == 4

    gu_pos, down_pos, ffn_order = stream_positions(NB)
    FU = len(ffn_order)

    units = []
    in_order = [4, 5, 6, 7, 0, 1, 2, 3]
    U_GIN = len(units)
    units += [("in", (A["ga_w_in"][0],), cb, h) for cb in in_order for h in range(2)]
    U_GOUT = len(units)
    units += [("out", (A["ga_w_out"][0],), i, 0) for i in range(KG // 2)]
    U_FFN = len(units)
    dense = (A["fd_w_gate"][0], A["fd_w_up"][0], A["fd_w_down"][0])
    units += [(kind, dense, b, h) for kind, b, h in ffn_order]
    U_PLE0 = len(units)
    units += [("out", (A["ple_w_proj"][0],), 0, 0)] + [("out", (A["ple_w_gate"][0],), i, 0) for i in range(KD // 2)]
    U_MIN = len(units)
    units += [("in", (A["mb_w_in"][0],), cb, h) for cb in range(8) for h in range(2)]
    U_MOUT = len(units)
    units += [("out", (A["mb_w_out"][0],), i, 0) for i in range(KI // 2)]
    U_MOE = len(units)
    U_PLE1 = U_MOE + E * FU
    ple1_units = [("out", (A["ple_w_proj"][1],), 0, 0)] + [("out", (A["ple_w_gate"][1],), i, 0) for i in range(KD // 2)]

    SLOTS = 11
    LENT = 2
    EARLY = SLOTS - LENT
    HIS = 3
    assert FU % SLOTS == 0 and FU % HIS == 0

    def slot_of(u):
        return u % EARLY if u < U_MOE else (u - U_MOE) % SLOTS

    early_uses = [len([u for u in range(U_MOE) if u % EARLY == s]) if s < EARLY else 0 for s in range(SLOTS)]

    def uses_before(u):
        if u < U_MOE:
            return u // EARLY
        return early_uses[slot_of(u)] + (u - U_MOE) // SLOTS

    with ExitStack() as ctx:
        base = (nc.sbuf_base + 31) // 32 * 32
        UNIT = 2048
        KB = 1024
        O_RING = 0
        O_HI = O_RING + SLOTS * 8 * KB
        O_X = O_HI + HIS * 8 * KB
        O_XN = O_X + 8 * KB
        O_HTH = O_XN + 8 * KB
        O_HTL = O_HTH + 8 * KB
        O_C = O_HTL + 8 * KB
        O_LENT = O_RING + EARLY * 8 * KB
        cursor = [O_C]

        def at(name, off, shape, dt=F32):
            return nc.alloc_sbuf_tensor_at(name, shape, dt, offset=base + off)

        def const(name, shape, dt=F32):
            n = 1
            for s in shape[1:]:
                n *= s
            t = at(name, cursor[0], shape, dt)
            cursor[0] += (4 * n + 31) // 32 * 32
            return t

        raw = at("raw_weights", O_RING, [P, SLOTS, UNIT])
        wlo = at("weights_lo", O_RING, [P, SLOTS, UNIT], F32R)
        whi = at("weights_hi", O_HI, [P, HIS, UNIT], F32R)
        x = at("x_res", O_X, [P, NT, D])
        xn = at("x_normed", O_XN, [P, NT, D])
        hTh = at("hT_hi", O_HTH, [P, KD, T], F32R)
        hTl = at("hT_lo", O_HTL, [P, KD, T], F32R)

        ident = const("ident", [P, P])
        tri_incl = const("tri_incl", [P, P])
        tri_strict = const("tri_strict", [P, P])
        ones = const("ones", [P, P])
        far = const("masked_far", [P, P])
        slot_iota = const("slot_iota", [P, P])
        earlier = const("earlier_expert", [P, E, E])
        own_block = const("own_block", [P, 32])
        vec_a = const("vec_a", [P, CONV * KI + 3 * KI])
        vec_b = const("vec_b", [P, 6 * KD])
        qkv_w = const("qkv_w", [P, 3, KI, QB])
        w_gate = const("w_gate", [P, 3 * KI, 2 * H])
        router = const("router", [P, KD, E])
        b_gate = const("b_gate", [1, 2 * H])
        ss = const("sum_squares", [P, NT])
        var = const("variance", [P, NT])
        rstd = const("rstd", [P, NT])
        newton = const("newton", [P, NT * H])
        ln_stats = const("ln_stats", [P, NT, 4, 6])
        ln_mv = const("ln_mv", [P, NT, 2])
        gates = const("gates", [P, NT, 2 * H])
        gate_t = const("gate_tmp", [P, NT, H])
        gate_e = const("gate_exp", [P, NT, H])
        logf = const("log_f", [P, NT, H])
        a_tok = const("a_tok", [P, NT, H])
        b_tok = const("b_tok", [P, NT, H])
        emt = const("exp_minus_m", [P, NT, H])
        qn = const("qn", [P, NT, H])
        head_stats = const("head_stats", [P, NT, H, 6])
        head_mv = const("head_mv", [P, NT, H, 2])
        head_r = const("head_r", [P, NT, H])
        head_v = const("head_v", [P, NT, H])
        head_s = const("head_s", [P, NT, H])
        logits = const("logits", [P, NT, E])
        rank = const("rank", [P, NT, E])
        sel = const("sel", [P, 2, NT, E])
        top = const("top", [P, 2, NT])
        prob = const("prob", [P, 2, NT])
        comb = const("combine", [P, NT, E])
        chosen = const("chosen", [P, NT, E])
        slot = const("slot_of_token", [P, NT, E])
        c_slot = const("slot_weight", [P, 1])
        most = const("most_tokens", [P, 1])
        over = const("over_flag", [P, 1], I32)
        O_PH = cursor[0]
        assert base + O_PH + 3 * 16 * KB + 4352 <= nc.sbuf_usable_end, (O_PH, nc.sbuf_usable_end)

        uT = at("uT", O_PH, [P, KG, T])
        glo = at("gated_lo", O_PH, [P, KG, T], F32R)
        rows_a = at("rows_a", O_PH, [P, P])
        rows_b = at("rows_b", O_PH + 512, [P, P])
        v = at("v_tok", O_PH + 16 * KB, [P, NT, GD])
        ghi = at("gated_hi", O_PH + 16 * KB, [P, NT, KG, P], F32R)
        w_s = at("w_spatial", O_PH + 32 * KB, [P, G, P])
        w_sT = at("w_spatialT", O_PH + 36 * KB, [P, G, P])
        b_s = at("b_spatial", O_PH + 40 * KB, [P, G, P])
        gtmp = at("gmlp_tmp", O_PH + 44 * KB, [P, 2, NT, P])
        ln_g = at("ln_g", O_LENT, [P, GD])
        ln_b = at("ln_b", O_LENT + 8 * KB, [P, GD])
        gprod = at("gmlp_prod", O_XN, [P, 2, 2, NT, P])
        xc = at("xc", O_LENT, [P, KI, T])
        qT = at("qT", O_PH, [P, KI, T])
        num = at("numerator", O_PH, [P, H, NT, DH])
        ohi = at("mixed_hi", O_PH, [P, KI, T], F32R)
        kT = at("kT", O_PH + 16 * KB, [P, KI, T])
        sz = at("sigmoid_z", O_PH + 16 * KB, [P, KI, T])
        olo = at("mixed_lo", O_PH + 16 * KB, [P, KI, T], F32R)
        v_m = at("v_mlstm", O_PH + 32 * KB, [P, NT, DI])
        xpad = at("xm_padded", O_PH + 48 * KB, [P, 4, CONV - 1 + T])
        blockdiag = at("blockdiag", O_XN, [P, 3, 4, P])
        vT = at("vT", O_XN + 6 * KB, [P, 2, T])
        ROW = P + T
        scan = [at(f"scan_{i}", O_PH + 48 * KB + i * 4 * ROW, [H, ROW]) for i in range(2)]
        arg = at("decay_arg", O_XN, [P, 3 * P])
        wexp = at("decay", O_XN + 1536, [P, 2, 3 * P])
        pT = at("pT_weights", O_XN + 4608, [P, 2, 3 * P])
        otmp = at("out_tmp", O_XN, [P, 2, 2, T])
        sg = at("silu_gate", O_PH, [P, 2, FB])
        hid = at("hidden", O_PH + 2 * KB, [P, 2, NT, FB])
        hidTh = at("hiddenT_hi", O_PH + 6 * KB, [P, 2, 2, T], F32R)
        hidTl = at("hiddenT_lo", O_PH + 10 * KB, [P, 2, 2, T], F32R)
        p_tok = at("p_tok", O_PH + 14 * KB, [P, NT, PLE])
        pTh = at("pT_hi", O_PH + 16 * KB, [P, KP, T], F32R)
        pTl = at("pT_lo", O_PH + 18 * KB, [P, KP, T], F32R)
        psig = at("ple_gate", O_PH + 20 * KB, [P, NT, D])
        hT32 = at("hT_full", O_HTH, [P, KD, T])
        hh = at("h_hi", O_PH + 28 * KB, [P, NT, D], F32R)
        hl = at("h_lo", O_PH + 36 * KB, [P, NT, D], F32R)
        g_row = at("gain_row", O_PH + 44 * KB, [P, D])
        cmp = at("rank_cmp", O_PH + 20 * KB, [P, 2, NT, E, E])
        xgh = at("gathered_hi", O_HTH, [P, KD, P], F32R)
        xgl = at("gathered_lo", O_HTL, [P, KD, P], F32R)
        pick = at("pick", O_PH + 48 * KB, [P, NT, P], F32R)
        pickT = at("pickT", O_PH + 49 * KB, [P, NT, P], F32R)
        yh = at("y_hi", O_PH + 20 * KB, [P, D], F32R)
        yl = at("y_lo", O_PH + 24 * KB, [P, D], F32R)

        o_gate = at("over_gate", O_PH, [P, KD, FB])
        o_up = at("over_up", O_HTL, [P, KD, FB])
        o_down = at("over_down", O_PH + 20 * KB, [P, 2, D])
        o_sg = at("over_silu", O_PH + 8 * KB, [P, FB])
        o_hid = at("over_hidden", O_PH + 9 * KB, [P, FB])
        o_hidT = at("over_hiddenT", O_PH + 10 * KB, [P, 2, P])
        o_y = at("over_y", O_PH + 16 * KB, [P, D])
        o_xg = at("over_gathered", O_HTH, [P, KD, P])
        o_pick = at("over_pick", O_PH + 48 * KB, [P, NT, P])
        o_pickT = at("over_pickT", O_PH + 49 * KB, [P, NT, P])

        ps = [ctx.enter_context(nc.psum_tensor(f"bank{i}", [P, 512], F32)) for i in range(8)]

        def sem(name):
            return ctx.enter_context(nc.semaphore(name))

        landed = [sem(f"landed_{s}") for s in range(SLOTS)]
        hi_ready = sem("hi_ready")
        lo_ready = sem("lo_ready")
        unit_used = sem("unit_used")
        lent_free = sem("lent_free")
        x_in = sem("x_in")
        rows_in = sem("rows_in")
        spatial_in = sem("spatial_in")
        ln_in = sem("ln_in")
        mlstm_in = sem("mlstm_in")
        p_in = [sem("p_in_0"), sem("p_in_1")]
        gain_in = sem("gain_in")
        final_in = sem("final_in")
        out_done = sem("out_done")
        pool_step = sem("pool_step")
        dve_step = sem("dve_step")
        act_step = sem("act_step")
        consts_ready = sem("consts_ready")
        prep_turned = sem("prep_turned")
        prep_copied = sem("prep_copied")
        gains_copied = sem("gains_copied")
        x_ready = sem("x_ready")
        squares = sem("squares")
        xn_ready = sem("xn_ready")
        turned = sem("turned")
        hi_turned = sem("hi_turned")
        h_ready = sem("h_ready")
        v_gelu = sem("v_gelu")
        v_normed = sem("v_normed")
        v_ready = sem("v_ready")
        u_gelu = sem("u_gelu")
        mixed = sem("mixed")
        gated = sem("gated")
        gated_hi = sem("gated_hi")
        gated_lo = sem("gated_lo")
        silu_done = sem("silu_done")
        hid_ready = sem("hid_ready")
        hid_turned = sem("hid_turned")
        hidT_hi = sem("hidT_hi")
        hidT_lo = sem("hidT_lo")
        p_turned = sem("p_turned")
        p_hi = sem("p_hi")
        p_ready = sem("p_ready")
        ple_sig = sem("ple_sig")
        bd_ready = sem("bd_ready")
        xm_copied = sem("xm_copied")
        conv_first = sem("conv_first")
        pad_ready = sem("pad_ready")
        conv_done = sem("conv_done")
        xc_ready = sem("xc_ready")
        qkv_mm = sem("qkv_mm")
        qk_copied = sem("qk_copied")
        v_copied = sem("v_copied")
        bd_used = sem("bd_used")
        gates_mm = sem("gates_mm")
        forget_in = sem("forget_in")
        forget_ln = sem("forget_ln")
        logf_ready = sem("logf_ready")
        cums_mm = sem("cums_mm")
        a_ready = sem("a_ready")
        a_turned = sem("a_turned")
        m_ready = sem("m_ready")
        m_turned = sem("m_turned")
        m_tok_ready = sem("m_tok_ready")
        emt_ready = sem("emt_ready")
        scores_mm = sem("scores_mm")
        arg_ready = sem("arg_ready")
        decay_ready = sem("decay_ready")
        p_weights = sem("p_weights")
        num_mm = sem("num_mm")
        num_copied = sem("num_copied")
        z_exp = sem("z_exp")
        z_ready = sem("z_ready")
        hn_ready = sem("hn_ready")
        hn_turned = sem("hn_turned")
        mixed_ready = sem("mixed_ready")
        mixed_hi = sem("mixed_hi")
        mixed_lo = sem("mixed_lo")
        h_gained = sem("h_gained")
        hh_ready = sem("hh_ready")
        hl_ready = sem("hl_ready")
        turned32 = sem("turned32")
        hT32_ready = sem("hT32_ready")
        logits_mm = sem("logits_mm")
        prob_exp = sem("prob_exp")
        chosen_ready = sem("chosen_ready")
        slots_mm = sem("slots_mm")
        slots_ready = sem("slots_ready")
        over_known = sem("over_known")
        o_picked = sem("o_picked")
        o_gathered = sem("o_gathered")
        o_copied = sem("o_copied")
        o_landed = sem("o_landed")
        o_gu_mm = sem("o_gu_mm")
        o_silu = sem("o_silu")
        o_hid_ready = sem("o_hid_ready")
        o_hid_turned = sem("o_hid_turned")
        o_hidT_ready = sem("o_hidT_ready")
        o_down_mm = sem("o_down_mm")
        o_y_added = sem("o_y_added")
        o_y_ready = sem("o_y_ready")
        o_back = sem("o_back")
        o_added = sem("o_added")
        e_pick = sem("e_pick")
        e_gathered = sem("e_gathered")
        e_xg_hi = sem("e_xg_hi")
        e_xg_lo = sem("e_xg_lo")
        e_pickT_mm = sem("e_pickT_mm")
        e_pickT = sem("e_pickT")
        e_pickT_c = sem("e_pickT_c")
        e_silu = sem("e_silu")
        e_hid = sem("e_hid")
        e_hid_turned = sem("e_hid_turned")
        e_hidT_hi = sem("e_hidT_hi")
        e_hidT_lo = sem("e_hidT_lo")
        e_y_hi = sem("e_y_hi")
        e_y_lo = sem("e_y_lo")
        e_back = sem("e_back")
        e_added = sem("e_added")

        block = ctx.enter_context(nc.Block())

        SPLIT_AT, PICK_AT, GATHER_AT = 4, 6, 8
        XR_GMLP, XR_FFN, XR_PLE0, XR_MLSTM, XR_MOE, XR_PLE1, XR_FINAL = range(7)

        def unit_parts(kind, tensors, i, h):
            if kind == "in":
                src = tensors[0][4 * h * P:(4 * h + 4) * P, i * CW:(i + 1) * CW].rearrange("(k p) n -> p k n", p=P)
                return [(lambda r, k=k: r.rearrange("p (k n) -> p k n", k=4)[:, k:k + 2, :], src[:, k:k + 2, :])
                        for k in (0, 2)]
            if kind in ("out", "down"):
                w = tensors[-1]
                src = w[2 * i * P:(2 * i + 2) * P, :].rearrange("(k p) n -> p k n", p=P)
                return [(lambda r, k=k: r.rearrange("p (k n) -> p k n", k=2)[:, k, :], src[:, k, :]) for k in (0, 1)]
            parts = []
            for j in (0, 1):
                src = tensors[j][4 * h * P:(4 * h + 4) * P, i * FB:(i + 1) * FB].rearrange("(k p) n -> p k n", p=P)
                parts.append((lambda r, j=j: r.rearrange("p (k j n) -> p k j n", k=4, j=2)[:, :, j, :], src))
            return parts

        @block.sync
        def _(sp):
            def load(s, unit):
                for dst, src in unit_parts(*unit):
                    sp.dma_start(dst(raw[:, s, :]), src).then_inc(landed[s], 16)

            sp.dma_start(x[:], A["x"][0].rearrange("(t p) d -> p t d", p=P)).then_inc(x_in, 16)
            for u in range(U_MOE):
                if u >= EARLY:
                    sp.wait_ge(unit_used, u - EARLY + 1)
                load(slot_of(u), units[u])

            def expert_unit(e, j):
                kind, b, h = ffn_order[j]
                return (kind, (A["fe_w_gate"][0, e], A["fe_w_up"][0, e], A["fe_w_down"][0, e]), b, h)

            for m in range(SLOTS):
                if m < EARLY:
                    sp.wait_ge(unit_used, max(u for u in range(U_MOE) if slot_of(u) == m) + 1)
                else:
                    sp.wait_ge(lent_free, 1)
                load(m, expert_unit(0, m))
            with sp.Fori(0, E - 1) as e:
                for j in range(SLOTS, SLOTS + FU):
                    sp.wait_ge(unit_used, e * FU + (U_MOE + j - SLOTS + 1))
                    load(j % SLOTS, expert_unit(e + 1 if j >= FU else e, j % FU))
            for j in range(SLOTS, FU):
                sp.wait_ge(unit_used, (E - 1) * FU + U_MOE + j - SLOTS + 1)
                load(j % SLOTS, expert_unit(E - 1, j))
            for i, unit in enumerate(ple1_units):
                sp.wait_ge(unit_used, U_PLE1 + i - SLOTS + 1)
                load(slot_of(U_PLE1 + i), unit)
            sp.wait_ge(out_done, 16 * NT)

        @block.gpsimd
        def _(pool):
            n = [0]

            def link(ins):
                n[0] += 1
                ins.then_inc(pool_step, 1)
                pool.wait_ge(pool_step, n[0])

            g = nc.gpsimd
            g.memset(ident[:], 0.0).then_inc(pool_step, 1)
            g.memset(ones[:], 1.0).then_inc(pool_step, 1)
            n[0] += 2
            pool.wait_ge(pool_step, n[0])
            link(g.affine_select(out=ident[:], in_=ident[:], compare_op=ALU.not_equal, fill=1.0, base=0,
                                 pattern=[[-1, P]], channel_multiplier=1))
            link(g.affine_select(out=tri_incl[:], in_=ones[:], compare_op=ALU.is_ge, fill=0.0, base=0,
                                 pattern=[[1, P]], channel_multiplier=-1))
            link(g.affine_select(out=tri_strict[:], in_=ones[:], compare_op=ALU.is_gt, fill=0.0, base=0,
                                 pattern=[[1, P]], channel_multiplier=-1))
            link(g.memset(far[:], 0.0))
            link(g.affine_select(out=far[:], in_=far[:], compare_op=ALU.is_ge, fill=BIG, base=0,
                                 pattern=[[1, P]], channel_multiplier=-1))
            link(g.iota(slot_iota[:], pattern=[[1, P]], base=0, channel_multiplier=0,
                        allow_small_or_imprecise_dtypes=True))
            link(g.memset(earlier[:], 1.0))
            link(g.affine_select(out=earlier[:], in_=earlier[:], compare_op=ALU.is_gt, fill=0.0, base=0,
                                 pattern=[[1, E], [-1, E]], channel_multiplier=0))
            link(g.memset(own_block[:], 1.0))
            link(g.affine_select(out=own_block[:], in_=own_block[:], compare_op=ALU.is_ge, fill=0.0, base=0,
                                 pattern=[[-QB, 32]], channel_multiplier=1))
            link(g.affine_select(out=own_block[:], in_=own_block[:], compare_op=ALU.is_ge, fill=0.0, base=QB - 1,
                                 pattern=[[QB, 32]], channel_multiplier=-1))
            pool.wait_ge(spatial_in, 32)
            g.memset(w_s[0:64, :, 64:P], 0.0).then_inc(consts_ready, 1)
            pool.wait_ge(ln_in, 32)
            for t in range(NT):
                pool.wait_ge(v_normed, t + 1)
                link(g.tensor_tensor(v[:, t, :], v[:, t, :], ln_g[:], ALU.mult))
                g.tensor_tensor(v[:, t, :], v[:, t, :], ln_b[:], ALU.add).then_inc(v_ready, 1)
            pool.wait_ge(mlstm_in, 16 * 5)
            pool.wait_ge(turned, 4 * (XR_MLSTM + 1))
            for i in range(KI // 4):
                if i:
                    pool.wait_ge(bd_used, i)
                for j in range(3):
                    o = blockdiag[:, j, :, :].rearrange("p c (m d) -> p c m d", d=QB)
                    for cc in range(4):
                        ins = g.tensor_tensor(
                            o[:, cc], qkv_w[:, j, 4 * i + cc, :].unsqueeze(1).to_broadcast([P, 32, QB]),
                            own_block[:].unsqueeze(2).to_broadcast([P, 32, QB]), ALU.mult)
                ins.then_inc(bd_ready, 1)

        @block.scalar
        def _(act):
            a = nc.scalar
            steps = [0]

            def link(ins):
                steps[0] += 1
                ins.then_inc(act_step, 1)
                act.wait_ge(act_step, steps[0])

            hi_next = [0]

            def split_hi(end):
                while hi_next[0] < end:
                    u = hi_next[0]
                    act.wait_ge(landed[slot_of(u)], 32 * (uses_before(u) + 1))
                    if u >= HIS:
                        act.wait_ge(unit_used, u - HIS + 1)
                    a.copy(whi[:, u % HIS, :], raw[:, slot_of(u), :]).then_inc(hi_ready, 1)
                    hi_next[0] += 1

            def rows(dst, r0, src):
                k = src.shape[0] // P
                act.dma_start(dst[r0:r0 + k, :], src.rearrange("(k p) -> k p", p=P)).then_inc(rows_in, 16)

            for j in range(CONV):
                rows(rows_a, KI * j, A["mb_conv_w"][0, j])
            for j, name in enumerate(("mb_conv_b", "mb_norm_g", "mb_skip")):
                rows(rows_a, KI * (CONV + j), A[name][0])
            for j in range(2):
                rows(rows_b, KD * j, A["norm_mix"][j])
                rows(rows_b, KD * (2 + j), A["norm_ffn"][j])
                rows(rows_b, KD * (4 + j), A["norm_ple"][j])
            act.dma_start(w_s[:], A["ga_w_s"][0].rearrange("g t s -> t g s")).then_inc(spatial_in, 16)
            act.dma_start(b_s[:], A["ga_b_s"][0].rearrange("g t -> (g t)").partition_broadcast(P)
                          .rearrange("p (g t) -> p g t", g=G)).then_inc(spatial_in, 16)
            act.dma_start(ln_g[:], A["ga_ln_g"][0].partition_broadcast(P)).then_inc(ln_in, 16)
            act.dma_start(ln_b[:], A["ga_ln_b"][0].partition_broadcast(P)).then_inc(ln_in, 16)
            for j, name in enumerate(("mb_wq", "mb_wk", "mb_wv")):
                act.dma_start(qkv_w[:, j, :, :], A[name][0].rearrange("(c n) i d -> (n i) c d", n=32)).then_inc(mlstm_in, 16)
            act.dma_start(w_gate[:], A["mb_w_gate"][0].rearrange("(k p) n -> p k n", p=P)).then_inc(mlstm_in, 16)
            act.dma_start(b_gate[:], A["mb_b_gate"]).then_inc(mlstm_in, 16)
            act.dma_start(router[:], A["fe_router"][0].rearrange("(k p) e -> p k e", p=P)).then_inc(gain_in, 16)

            def normalise(r):
                if r:
                    act.wait_ge(x_ready, r)
                else:
                    act.wait_ge(x_in, 16)
                a.activation(xn[:, 0, :], x[:, 0, :], ACT.Square, accum_out=ss[:, 0:1]).then_inc(squares, 1)

            def turn_hi(r, g0):
                for kp in range(KD // 2):
                    act.wait_ge(turned, (KD // 2) * r + kp + 1)
                    for k in (0, 1):
                        ins = a.activation(hTh[:, 2 * kp + k, :], ps[4 + kp][:, T * k:T * (k + 1)], ACT.Copy,
                                           scale=vec_b[:, g0 + 2 * kp + k:g0 + 2 * kp + k + 1])
                    ins.then_inc(hi_turned, 1)

            normalise(XR_GMLP)
            act.wait_ge(prep_turned, 2)
            a.copy(vec_b[:], ps[1][:, 0:6 * KD]).then_inc(gains_copied, 1)
            act.wait_ge(gains_copied, 1)
            turn_hi(XR_GMLP, 0)
            split_hi(U_GIN + 3)
            for i in range(4):
                act.wait_ge(unit_used, U_GIN + 2 * i + 2)
                split_hi(U_GIN + 2 * i + 4)
                for t in range(NT):
                    a.activation(v[:, t, i * CW:(i + 1) * CW], ps[2 * (i % 2) + t][:], ACT.Gelu).then_inc(v_gelu, 1)
                split_hi(U_GIN + 2 * i + 5)
            for i in range(4):
                un = U_GIN + 8 + 2 * i + 2
                act.wait_ge(unit_used, un)
                split_hi(un + 2)
                for b in range(2):
                    a.activation(uT[:, 4 * i + 2 * b:4 * i + 2 * b + 2, :], ps[2 * (i % 2) + b][:], ACT.Gelu).then_inc(u_gelu, 1)
                split_hi(un + 3)
            for g in range(G):
                act.wait_ge(gated, g + 1)
                a.copy(ghi[:, :, 2 * g:2 * g + 2, :],
                       gprod[:, g % 2].rearrange("p c n t -> p n c t")).then_inc(gated_hi, 1)
                split_hi(min(U_GOUT + g + 3, U_FFN))
            split_hi(U_FFN + 1)

            normalise(XR_FFN)
            turn_hi(XR_FFN, 2 * KD)
            split_hi(U_FFN + 3)

            def ffn_hi(base_unit):
                act.dma_start(p_tok[:], A["p"][0, 0].rearrange("(t p) n -> p t n", p=P)).then_inc(p_in[0], 16)
                for b in range(NB + 2):
                    if b < NB:
                        un = base_unit + gu_pos[b] + 2
                        split_hi(un + 1)
                        act.wait_ge(unit_used, un)
                        for t in range(NT):
                            a.activation(sg[:, t, :], ps[t][:, 0:FB], ACT.Silu).then_inc(silu_done, 1)
                        split_hi(un + 2)
                    if 1 <= b <= NB:
                        act.wait_ge(hid_turned, b)
                        a.copy(hidTh[:, (b - 1) % 2].rearrange("p j t -> p (j t)"), ps[2][:]).then_inc(hidT_hi, 1)
                    if b >= 2:
                        split_hi(base_unit + down_pos[b - 2] + 2)

            ffn_hi(U_FFN)

            def ple(l, r, base_unit, g0):
                act.wait_ge(p_turned, l + 1)
                a.copy(pTh[:].rearrange("p k t -> p (k t)"), ps[3][:]).then_inc(p_hi, 1)
                split_hi(base_unit + 3)
                normalise(r)
                turn_hi(r, g0)
                for i in range(1, 5):
                    split_hi(min(base_unit + i + 3, base_unit + 5))
                act.wait_ge(unit_used, base_unit + 5)
                for t in range(NT):
                    for h in range(2):
                        a.activation(psig[:, t, h * CW:(h + 1) * CW], ps[4 + 2 * t + h][:], ACT.Sigmoid).then_inc(ple_sig, 1)

            ple(0, XR_PLE0, U_PLE0, 4 * KD)
            split_hi(U_MIN + 1)

            def mlstm():
                normalise(XR_MLSTM)
                turn_hi(XR_MLSTM, KD)
                split_hi(U_MIN + 3)

                def copy_qk(i):
                    for pr in range(2):
                        for j, dst in enumerate((qT, kT)):
                            item = (2 * i + pr) * 4 + j
                            act.wait_ge(qkv_mm, item + 1)
                            c = 4 * i + 2 * pr
                            a.copy(dst[:, c:c + 2, :].rearrange("p c t -> p (c t)"), ps[4 + item % 3][:]).then_inc(qk_copied, 1)

                for i in range(4):
                    un = U_MIN + 2 * i + 2
                    act.wait_ge(unit_used, un)
                    split_hi(un + 2)
                    if i:
                        copy_qk(i - 1)
                        act.wait_ge(bd_used, i)
                    split_hi(un + 3)
                    if not i:
                        act.wait_ge(pad_ready, 1)
                    for b in range(2):
                        ins = a.copy(xpad[:, 2 * b:2 * b + 2, CONV - 1:], ps[2 * (i % 2) + b][:].rearrange("p (c t) -> p c t", c=2))
                    ins.then_inc(xm_copied, 1)
                    act.wait_ge(xm_copied, i + 1)
                    for cc in range(4):
                        c = 4 * i + cc
                        ins = a.activation(xc[:, c, :], xpad[:, cc, 0:T], ACT.Identity, scale=vec_a[:, c:c + 1],
                                           bias=vec_a[:, CONV * KI + c:CONV * KI + c + 1])
                    ins.then_inc(conv_first, 1)
                    act.wait_ge(conv_done, i + 1)
                    a.activation(xc[:, 4 * i:4 * i + 4, :], xc[:, 4 * i:4 * i + 4, :], ACT.Silu).then_inc(xc_ready, 1)
                copy_qk(3)
                act.wait_ge(forget_in, 1)
                link(a.activation(gate_e[:], gate_t[:], ACT.Exp))
                a.activation(gate_t[:], gate_e[:], ACT.Ln, bias=1.0).then_inc(forget_ln, 1)
                un = U_MIN + 8
                split_hi(un + 2)
                act.wait_ge(unit_used, un + 1)
                split_hi(un + 4)
                act.wait_ge(m_tok_ready, 1)
                a.activation(emt[:], emt[:], ACT.Exp, scale=-1.0).then_inc(emt_ready, 1)

                def decay(h):
                    act.wait_ge(arg_ready, h + 1)
                    if h >= 2:
                        act.wait_ge(p_weights, h - 1)
                    a.activation(wexp[:, h % 2, :], arg[:], ACT.Exp, scale=-1.0).then_inc(decay_ready, 1)

                def take_num(h):
                    act.wait_ge(num_mm, h + 1)
                    a.copy(num[:, h].rearrange("p t d -> p (t d)"), ps[2][:]).then_inc(num_copied, 1)

                for i in range(4):
                    un = U_MIN + 8 + 2 * i + 2
                    act.wait_ge(unit_used, un)
                    split_hi(min(un + 2, U_MOUT + 2))
                    for h in (2 * i, 2 * i + 1):
                        decay(h)
                        if h:
                            take_num(h - 1)
                    act.wait_ge(scores_mm, 2 * i + 2)
                    for b in range(2):
                        a.activation(sz[:, 4 * i + 2 * b:4 * i + 2 * b + 2, :].rearrange("p c t -> p (c t)"), ps[b][:],
                                     ACT.Exp, scale=-1.0).then_inc(z_exp, 1)
                    split_hi(min(un + 3, U_MOUT + 2))
                take_num(H - 1)
                act.wait_ge(num_mm, H + 1)
                a.copy(qn[:].rearrange("p t h -> p (t h)"), ps[3][:, 0:NT * H]).then_inc(num_copied, 1)
                for g in range(H):
                    act.wait_ge(mixed_ready, g + 1)
                    a.copy(ohi[:, 2 * g:2 * g + 2, :], otmp[:, g % 2]).then_inc(mixed_hi, 1)
                    split_hi(min(U_MOUT + g + 3, U_MOE))
                split_hi(U_MOE + 1)

            mlstm()

            def experts():
                act.dma_start(g_row[:], A["norm_ffn"][1].partition_broadcast(P)).then_inc(gain_in, 16)
                normalise(XR_MOE)
                act.wait_ge(h_gained, 1)
                a.copy(hh[:], xn[:]).then_inc(hh_ready, 1)
                for kp in range(4):
                    act.wait_ge(turned, 4 * XR_MOE + kp + 1)
                    a.copy(hT32[:, 2 * kp:2 * kp + 2, :].rearrange("p k t -> p (k t)"), ps[4 + kp][:]).then_inc(hT32_ready, 1)
                split_hi(U_MOE + 3)
                act.wait_ge(chosen_ready, 1)
                a.activation(prob[:, 0, :], top[:, 0, :], ACT.Exp).then_inc(prob_exp, 1)
                act.dma_start(p_tok[:], A["p"][1, 0].rearrange("(t p) n -> p t n", p=P)).then_inc(p_in[1], 16)

                act.wait_ge(over_known, 1)
                with act.If(act.value_load(over[0:1, 0:1], min_val=0, max_val=1) > 0):
                    with act.Fori(0, E) as e:
                        with act.Fori(0, NB) as b:
                            act.wait_ge(o_y_added, e * NB + b + 1)
                            for w, dst in (("fe_w_gate", o_gate), ("fe_w_up", o_up)):
                                act.dma_start(dst[:], A[w][0, e].rearrange("(k p) f -> p k f", p=P)[:, :, bass.ds(b * FB, FB)]
                                              ).then_inc(o_landed, 16)
                            act.dma_start(o_down[:], A["fe_w_down"][0, e].rearrange("(f k p) n -> f p k n", k=2, p=P)[b]
                                          ).then_inc(o_landed, 16)
                            act.wait_ge(o_gu_mm, e * NB + b + 1)
                            a.activation(o_sg[:], ps[0][:, 0:FB], ACT.Silu).then_inc(o_silu, 1)
                    act.wait_ge(o_added, 4 * E)

                def gathered_hi(e, o):
                    for b in range(2):
                        act.wait_ge(e_gathered, e * 2 + (2 * o + b + 1))
                        a.copy(xgh[:, 4 * b:4 * b + 4, :].rearrange("p k s -> p (k s)"), ps[6 + b][:]).then_inc(e_xg_hi, 1)

                def y_hi(e):
                    act.wait_ge(unit_used, e * FU + (U_MOE + FU))
                    for b in range(2):
                        a.activation(yh[:, b * CW:(b + 1) * CW], ps[4 + b][:], ACT.Copy, scale=c_slot[:, 0:1]).then_inc(e_y_hi, 1)

                def blocks(e, o, span, more):
                    def split_e(end):
                        while hi_next[0] < end + o * FU:
                            j = hi_next[0]
                            s = j % SLOTS
                            act.wait_ge(landed[s], e * (32 * FU // SLOTS) + 32 * (early_uses[s] + j // SLOTS + 1))
                            act.wait_ge(unit_used, e * FU + (U_MOE + j - HIS + 1))
                            a.copy(whi[:, (U_MOE + j) % HIS, :], raw[:, s, :]).then_inc(hi_ready, 1)
                            hi_next[0] += 1

                    for b in span:
                        if b < NB:
                            un = gu_pos[b] + 2
                            split_e(un + 2)
                            act.wait_ge(unit_used, e * FU + (U_MOE + o * FU + un))
                            a.activation(sg[:, b % 2, :], ps[b % 2][:, 0:FB], ACT.Silu).then_inc(e_silu, 1)
                        if 1 <= b <= NB:
                            act.wait_ge(e_hid_turned, e * NB + (o * NB + b))
                            a.copy(hidTh[:, (b - 1) % 2, :, 0:P], ps[2][:, 0:2 * P].rearrange("p (j t) -> p j t", j=2)).then_inc(e_hidT_hi, 1)
                        if b == NB and more:
                            gathered_hi(e, o + 1)
                        if b == SPLIT_AT - 1:
                            act.wait_ge(e_pickT_mm, e + (o + 1))
                            a.copy(pickT[:].rearrange("p t s -> p (t s)"), ps[3][:, 0:T]).then_inc(e_pickT, 1)
                        if b >= NB:
                            split_e(down_pos[b - 2] + 3)

                gathered_hi(0, 0)
                hi_next[0] = HIS
                blocks(0, 0, range(SPLIT_AT), True)
                start = hi_next[0]
                with act.Fori(0, E - 1) as e:
                    hi_next[0] = start
                    blocks(e, 0, range(SPLIT_AT, NB + 2), True)
                    y_hi(e)
                    blocks(e, 1, range(SPLIT_AT), True)
                assert hi_next[0] == start + FU
                hi_next[0] = start
                blocks(E - 1, 0, range(SPLIT_AT, NB + 2), False)
                y_hi(E - 1)
                hi_next[0] += U_MOE + (E - 1) * FU

            experts()
            ple(1, XR_PLE1, U_PLE1, 5 * KD)
            act.dma_start(g_row[:], A["norm_final"].partition_broadcast(P)).then_inc(final_in, 16)
            normalise(XR_FINAL)
            for t in range(NT):
                act.wait_ge(xn_ready, 2 * XR_FINAL + t + 1)
                act.dma_start(out[0, t * P:(t + 1) * P, :], xn[:, t, :]).then_inc(out_done, 16)

        @block.vector
        def _(dve):
            d = nc.vector
            steps = [0]

            def link(ins):
                steps[0] += 1
                ins.then_inc(dve_step, 1)
                dve.wait_ge(dve_step, steps[0])

            lo_next = [0]

            def split_lo(end):
                while lo_next[0] < end:
                    u = lo_next[0]
                    dve.wait_ge(hi_ready, u + 1)
                    d.tensor_tensor(wlo[:, slot_of(u), :], raw[:, slot_of(u), :], whi[:, u % HIS, :].bitcast(F32),
                                    ALU.subtract).then_inc(lo_ready, 1)
                    lo_next[0] += 1

            def rsqrt(y, v_in, tmp):
                link(d.tensor_scalar(y.bitcast(I32), v_in.bitcast(I32), -0.5, RSQRT_SEED, ALU.mult, ALU.add))
                for _ in range(4):
                    link(d.tensor_tensor(tmp, y, y, ALU.mult))
                    link(d.tensor_tensor(tmp, tmp, v_in, ALU.mult))
                    link(d.tensor_scalar(tmp, tmp, -0.5, 1.5, ALU.mult, ALU.add))
                    link(d.tensor_tensor(y, y, tmp, ALU.mult))

            def normalise(r):
                if r:
                    dve.wait_ge(x_ready, r)
                else:
                    dve.wait_ge(x_in, 16)
                link(d.tensor_tensor_reduce(xn[:, 1, :], x[:, 1, :], x[:, 1, :], 1.0, 0.0, ALU.mult, ALU.add, ss[:, 1:2]))
                dve.wait_ge(squares, r + 1)
                link(d.tensor_scalar(var[:], ss[:], 1.0 / D, EPS, ALU.mult, ALU.add))
                rsqrt(rstd[:], var[:], newton[:, 0:NT])
                for t in range(NT):
                    if r == XR_FINAL:
                        link(d.tensor_scalar(xn[:, t, :], x[:, t, :], rstd[:, t:t + 1], None, ALU.mult))
                        dve.wait_ge(final_in, 16)
                        d.tensor_tensor(xn[:, t, :], xn[:, t, :], g_row[:], ALU.mult).then_inc(xn_ready, 1)
                    elif r == XR_MOE:
                        link(d.tensor_scalar(xn[:, t, :], x[:, t, :], rstd[:, t:t + 1], None, ALU.mult))
                        dve.wait_ge(gain_in, 32)
                        d.tensor_tensor(xn[:, t, :], xn[:, t, :], g_row[:], ALU.mult).then_inc(xn_ready, 1)
                    else:
                        d.tensor_scalar(xn[:, t, :], x[:, t, :], rstd[:, t:t + 1], None, ALU.mult).then_inc(xn_ready, 1)

            def turn_lo(r, g0, nth):
                for kp in range(KD // 2):
                    dve.wait_ge(hi_turned, (KD // 2) * nth + kp + 1)
                    for k in (0, 1):
                        kk = 2 * kp + k
                        ins = d.scalar_tensor_tensor(out=hTl[:, kk, :], in0=ps[4 + kp][:, T * k:T * (k + 1)],
                                                     scalar=vec_b[:, g0 + kk:g0 + kk + 1], in1=hTh[:, kk, :].bitcast(F32),
                                                     op0=ALU.mult, op1=ALU.subtract)
                    ins.then_inc(h_ready, 1)

            def add_to_x(last=True):
                for t in range(NT):
                    for h in range(2):
                        ins = d.tensor_tensor(x[:, t, h * CW:(h + 1) * CW], x[:, t, h * CW:(h + 1) * CW],
                                              ps[4 + 2 * t + h][:], ALU.add)
                ins.then_inc(x_ready, 1)

            normalise(XR_GMLP)
            dve.wait_ge(prep_turned, 4)
            d.tensor_copy(w_sT[:, 0:4, :].rearrange("p g t -> p (g t)"), ps[2][:]).then_inc(prep_copied, 1)
            d.tensor_copy(w_sT[:, 4:8, :].rearrange("p g t -> p (g t)"), ps[3][:]).then_inc(prep_copied, 1)
            d.tensor_copy(vec_a[:], ps[0][:, 0:(CONV + 3) * KI]).then_inc(prep_copied, 1)
            dve.wait_ge(prep_copied, 3)
            dve.wait_ge(gains_copied, 1)
            turn_lo(XR_GMLP, 0, 0)
            split_lo(U_GIN + 3)
            for i in range(4):
                split_lo(U_GIN + 2 * i + 4)
                for t in range(NT):
                    dve.wait_ge(v_gelu, NT * i + t + 1)
                    ins = d.bn_stats(ln_stats[:, t, i, :], v[:, t, i * CW:(i + 1) * CW])
                link(ins)
                split_lo(U_GIN + 2 * i + 5)
            for t in range(NT):
                link(d.bn_aggr(ln_mv[:, t, :], ln_stats[:, t].rearrange("p i s -> p (i s)")))
            link(d.tensor_scalar(var[:], ln_mv[:, :, 1], EPS, None, ALU.add))
            rsqrt(rstd[:], var[:], newton[:, 0:NT])
            for t in range(NT):
                d.tensor_scalar(v[:, t, :], v[:, t, :], ln_mv[:, t, 0:1], rstd[:, t:t + 1],
                                ALU.subtract, ALU.mult).then_inc(v_normed, 1)
            for i in range(4):
                split_lo(U_GIN + 8 + 2 * i + 5)
            for g in range(G):
                dve.wait_ge(mixed, g + 1)
                link(d.tensor_tensor(gtmp[:].rearrange("p c n t -> p (c n) t"), ps[4 + g % 4][:].rearrange("p (c t) -> p c t", c=4),
                                     b_s[:, g, :].unsqueeze(1).to_broadcast([P, 4, P]), ALU.add))
                dve.wait_ge(u_gelu, 8)
                d.tensor_tensor(gprod[:, g % 2].rearrange("p c n t -> p (c n t)"), gtmp[:].rearrange("p c n t -> p (c n t)"),
                                uT[:, 2 * g:2 * g + 2, :].rearrange("p c t -> p (c t)"), ALU.mult).then_inc(gated, 1)
                dve.wait_ge(gated_hi, g + 1)
                d.tensor_tensor(glo[:, 2 * g:2 * g + 2, :].rearrange("p c (n t) -> p c n t", n=NT).rearrange("p c n t -> p n c t"),
                                gprod[:, g % 2].rearrange("p c n t -> p n c t"),
                                ghi[:, :, 2 * g:2 * g + 2, :].bitcast(F32), ALU.subtract).then_inc(gated_lo, 1)
                split_lo(min(U_GOUT + g + 3, U_FFN))
            split_lo(U_FFN + 1)
            dve.wait_ge(unit_used, U_FFN)
            add_gmlp = add_to_x_banks(d, x, ps, 0, CW, NT)
            add_gmlp.then_inc(x_ready, 1)

            normalise(XR_FFN)
            turn_lo(XR_FFN, 2 * KD, 1)
            split_lo(U_FFN + 3)
            for b in range(NB + 2):
                if b < NB:
                    un = U_FFN + gu_pos[b] + 2
                    split_lo(un + 1)
                    for t in range(NT):
                        dve.wait_ge(silu_done, NT * b + t + 1)
                        d.tensor_tensor(hid[:, b % 2, t, :], sg[:, t, :], ps[t][:, FB:2 * FB], ALU.mult).then_inc(hid_ready, 1)
                    split_lo(un + 2)
                if 1 <= b <= NB:
                    dve.wait_ge(hidT_hi, b)
                    d.tensor_tensor(hidTl[:, (b - 1) % 2].rearrange("p j t -> p (j t)"), ps[2][:],
                                    hidTh[:, (b - 1) % 2].rearrange("p j t -> p (j t)").bitcast(F32), ALU.subtract).then_inc(hidT_lo, 1)
                if b >= 2:
                    split_lo(U_FFN + down_pos[b - 2] + 2)
            dve.wait_ge(unit_used, U_PLE0)
            add_to_x()

            def ple(l, r, base_unit, g0, nth):
                dve.wait_ge(p_hi, l + 1)
                d.tensor_tensor(pTl[:].rearrange("p k t -> p (k t)"), ps[3][:],
                                pTh[:].rearrange("p k t -> p (k t)").bitcast(F32), ALU.subtract).then_inc(p_ready, 1)
                split_lo(base_unit + 3)
                normalise(r)
                turn_lo(r, g0, nth)
                split_lo(base_unit + 5)
                for t in range(NT):
                    for h in range(2):
                        dve.wait_ge(ple_sig, 4 * l + 2 * t + h + 1)
                        s = psig[:, t, h * CW:(h + 1) * CW]
                        link(d.tensor_tensor(s, s, ps[2 * t + h][:], ALU.mult))
                        xs = x[:, t, h * CW:(h + 1) * CW]
                        ins = d.tensor_tensor(xs, xs, s, ALU.add)
                ins.then_inc(x_ready, 1)

            ple(0, XR_PLE0, U_PLE0, 4 * KD, 2)
            split_lo(U_MIN + 1)

            def mlstm():
                normalise(XR_MLSTM)
                turn_lo(XR_MLSTM, KD, 3)
                d.memset(xpad[:, :, 0:CONV - 1], 0.0).then_inc(pad_ready, 1)
                split_lo(U_MIN + 3)

                def copy_v(i):
                    for pr in range(2):
                        c = 4 * i + 2 * pr
                        item = (2 * i + pr) * 4 + 2
                        dve.wait_ge(qkv_mm, item + 1)
                        d.tensor_copy(vT[:].rearrange("p c t -> p (c t)"), ps[4 + item % 3][:]).then_inc(v_copied, 1)
                        dve.wait_ge(qkv_mm, item + 2)
                        d.tensor_copy(v_m[:, :, c * P:(c + 2) * P], ps[4 + (item + 1) % 3][:].rearrange("p (t f) -> p t f", t=NT)).then_inc(v_copied, 1)

                for i in range(4):
                    un = U_MIN + 2 * i + 2
                    split_lo(un + 2)
                    if i:
                        copy_v(i - 1)
                    split_lo(un + 3)
                    dve.wait_ge(conv_first, i + 1)
                    for j in range(1, CONV):
                        for cc in range(4):
                            c = 4 * i + cc
                            ins = d.scalar_tensor_tensor(out=xc[:, c, :], in0=xpad[:, cc, j:j + T],
                                                         scalar=vec_a[:, KI * j + c:KI * j + c + 1], in1=xc[:, c, :],
                                                         op0=ALU.mult, op1=ALU.add)
                        if j < CONV - 1:
                            link(ins)
                    ins.then_inc(conv_done, 1)
                copy_v(3)
                dve.wait_ge(gates_mm, 1)
                link(d.tensor_copy(gates[:].rearrange("p t g -> p (t g)"), ps[7][:, 0:NT * 2 * H]))
                link(d.tensor_scalar(gate_t[:], gates[:, :, H:], -1.0, None, ALU.mult))
                d.tensor_tensor(gate_t[:], gate_t[:], gates[:, :, H:], ALU.min).then_inc(forget_in, 1)
                for i in range(2):
                    d.memset(scan[i][:, 0:P], 0.0).then_inc(dve_step, 1)
                steps[0] += 2
                split_lo(U_MIN + 10)
                dve.wait_ge(forget_ln, 1)
                d.scalar_tensor_tensor(out=logf[:], in0=gates[:, :, H:], scalar=0.0, in1=gate_t[:],
                                       op0=ALU.min, op1=ALU.subtract).then_inc(logf_ready, 1)
                dve.wait_ge(cums_mm, 1)
                link(d.tensor_copy(b_tok[:].rearrange("p t h -> p (t h)"), ps[7][:, 64:64 + NT * H]))
                d.tensor_tensor(a_tok[:], gates[:, :, 0:H], b_tok[:], ALU.subtract).then_inc(a_ready, 1)
                split_lo(U_MIN + 11)
                dve.wait_ge(a_turned, 1)
                link(d.tensor_copy(scan[0][:, P:], ps[7][0:H, 256:256 + T]))
                cur = 0
                s = 1
                while s < T:
                    ins = d.tensor_tensor(scan[1 - cur][:, P:], scan[cur][:, P:], scan[cur][:, P - s:P - s + T], ALU.max)
                    cur = 1 - cur
                    s *= 2
                    if s < T:
                        link(ins)
                assert cur == 0
                ins.then_inc(m_ready, 1)
                split_lo(U_MIN + 12)
                dve.wait_ge(m_turned, 1)
                d.tensor_tensor(emt[:], b_tok[:], ps[7][:, 96:96 + NT * H].rearrange("p (t h) -> p t h", t=NT), ALU.add).then_inc(m_tok_ready, 1)

                def decay(h):
                    dve.wait_ge(scores_mm, h + 1)
                    if h:
                        dve.wait_ge(decay_ready, h)
                    mb = ps[6 + h % 2]
                    d.scalar_tensor_tensor(out=arg[:, 0:P], in0=mb[:, 0:P], scalar=a_tok[:, 0, h:h + 1], in1=far[:],
                                           op0=ALU.subtract, op1=ALU.max)
                    d.tensor_scalar(arg[:, P:2 * P], mb[:, P:2 * P], a_tok[:, 0, h:h + 1], 0.0, ALU.subtract, ALU.max)
                    d.scalar_tensor_tensor(out=arg[:, 2 * P:], in0=mb[:, P:2 * P], scalar=a_tok[:, 1, h:h + 1], in1=far[:],
                                           op0=ALU.subtract, op1=ALU.max).then_inc(arg_ready, 1)
                    dve.wait_ge(decay_ready, h + 1)
                    if h >= 2:
                        dve.wait_ge(num_mm, h - 1)
                    d.scalar_tensor_tensor(out=pT[:, h % 2, :], in0=ps[4 + h % 2][:, 0:3 * P], scalar=DH ** -0.5,
                                           in1=wexp[:, h % 2, :], op0=ALU.mult, op1=ALU.mult).then_inc(p_weights, 1)

                def stats(h):
                    dve.wait_ge(num_copied, h + 1)
                    for t in range(NT):
                        ins = d.bn_stats(head_stats[:, t, h, :], num[:, h, t, :])
                    link(ins)
                    for t in range(NT):
                        ins = d.bn_aggr(head_mv[:, t, h, :], head_stats[:, t, h, :])
                    link(ins)

                for i in range(4):
                    un = U_MIN + 8 + 2 * i + 2
                    split_lo(min(un + 2, U_MOUT + 2))
                    for h in (2 * i, 2 * i + 1):
                        decay(h)
                        if h:
                            stats(h - 1)
                    for b in range(2):
                        dve.wait_ge(z_exp, 2 * i + b + 1)
                        zz = sz[:, 4 * i + 2 * b:4 * i + 2 * b + 2, :]
                        link(d.tensor_scalar(zz, zz, 1.0, None, ALU.add))
                        d.reciprocal(zz, zz).then_inc(z_ready, 1)
                    split_lo(min(un + 3, U_MOUT + 2))
                for c in range(KI):
                    ins = d.tensor_scalar(xc[:, c, :], xc[:, c, :], vec_a[:, (CONV + 2) * KI + c:(CONV + 2) * KI + c + 1], None, ALU.mult)
                link(ins)
                stats(H - 1)
                dve.wait_ge(num_copied, H + 1)
                dve.wait_ge(emt_ready, 1)
                link(d.scalar_tensor_tensor(out=head_r[:], in0=qn[:], scalar=-1.0, in1=emt[:], op0=ALU.mult, op1=ALU.max))
                link(d.tensor_tensor(head_r[:], head_r[:], qn[:], ALU.max))
                link(d.reciprocal(head_r[:], head_r[:]))
                link(d.tensor_tensor(head_v[:], head_r[:], head_r[:], ALU.mult))
                link(d.tensor_tensor(head_v[:], head_v[:], head_mv[:, :, :, 1], ALU.mult))
                link(d.tensor_scalar(head_v[:], head_v[:], EPS, None, ALU.add))
                rsqrt(head_s[:], head_v[:], newton[:].rearrange("p (t h) -> p t h", t=NT))
                link(d.tensor_tensor(head_s[:], head_s[:], head_r[:], ALU.mult))
                for h in range(H):
                    for t in range(NT):
                        ins = d.tensor_scalar(num[:, h, t, :], num[:, h, t, :], head_mv[:, t, h, 0:1], head_s[:, t, h:h + 1],
                                              ALU.subtract, ALU.mult)
                    ins.then_inc(hn_ready, 1)
                for g in range(H):
                    dve.wait_ge(hn_turned, g + 1)
                    for k in range(2):
                        c = 2 * g + k
                        ins = d.scalar_tensor_tensor(out=otmp[:, g % 2, k, :], in0=ps[4 + g % 4][:, k * T:(k + 1) * T],
                                                     scalar=vec_a[:, (CONV + 1) * KI + c:(CONV + 1) * KI + c + 1], in1=xc[:, c, :],
                                                     op0=ALU.mult, op1=ALU.add)
                    if g == H - 1:
                        ins.then_inc(lent_free, 1)
                        dve.wait_ge(lent_free, 1)
                    else:
                        link(ins)
                    dve.wait_ge(z_ready, 8)
                    d.tensor_tensor(otmp[:, g % 2], otmp[:, g % 2], sz[:, 2 * g:2 * g + 2, :], ALU.mult).then_inc(mixed_ready, 1)
                    dve.wait_ge(mixed_hi, g + 1)
                    d.tensor_tensor(olo[:, 2 * g:2 * g + 2, :], otmp[:, g % 2], ohi[:, 2 * g:2 * g + 2, :].bitcast(F32),
                                    ALU.subtract).then_inc(mixed_lo, 1)
                    split_lo(min(U_MOUT + g + 3, U_MOE))
                split_lo(U_MOE + 1)
                dve.wait_ge(unit_used, U_MOE)
                add_to_x_banks(d, x, ps, 0, CW, NT).then_inc(x_ready, 1)

            mlstm()

            def experts():
                normalise(XR_MOE)
                dve.wait_ge(xn_ready, 2 * XR_MOE + 2)
                d.tensor_copy(rstd[:], rstd[:]).then_inc(h_gained, 1)
                dve.wait_ge(hh_ready, 1)
                d.tensor_tensor(hl[:], xn[:], hh[:].bitcast(F32), ALU.subtract).then_inc(hl_ready, 1)
                split_lo(U_MOE + 3)
                dve.wait_ge(logits_mm, 1)
                link(d.tensor_copy(logits[:].rearrange("p t e -> p (t e)"), ps[0][:, 0:NT * E]))
                lj = logits[:].unsqueeze(2).to_broadcast([P, NT, E, E])
                le = logits[:].unsqueeze(3).to_broadcast([P, NT, E, E])
                link(d.tensor_tensor(cmp[:, 0], lj, le, ALU.is_gt))
                link(d.tensor_tensor(cmp[:, 1], lj, le, ALU.is_equal))
                for t in range(NT):
                    ins = d.tensor_tensor(cmp[:, 1, t], cmp[:, 1, t], earlier[:], ALU.mult)
                link(ins)
                link(d.tensor_tensor(cmp[:, 0], cmp[:, 0], cmp[:, 1], ALU.add))
                link(d.tensor_reduce(rank[:], cmp[:, 0], AX.X, ALU.add))
                for j in range(2):
                    link(d.tensor_scalar(sel[:, j], rank[:], float(j), None, ALU.is_equal))
                    link(d.tensor_tensor(comb[:], sel[:, j], logits[:], ALU.mult))
                    link(d.tensor_reduce(top[:, j, :], comb[:], AX.X, ALU.add))
                link(d.tensor_tensor(chosen[:], sel[:, 0], sel[:, 1], ALU.add))
                d.tensor_tensor(top[:, 0, :], top[:, 1, :], top[:, 0, :], ALU.subtract).then_inc(chosen_ready, 1)
                dve.wait_ge(prob_exp, 1)
                link(d.tensor_scalar(prob[:, 1, :], prob[:, 0, :], 1.0, None, ALU.add))
                link(d.reciprocal(top[:, 0, :], prob[:, 1, :]))
                link(d.tensor_tensor(top[:, 1, :], top[:, 0, :], prob[:, 0, :], ALU.mult))
                for j in range(2):
                    for t in range(NT):
                        ins = d.tensor_scalar(sel[:, j, t, :], sel[:, j, t, :], top[:, j, t:t + 1], None, ALU.mult)
                    link(ins)
                link(d.tensor_tensor(comb[:], sel[:, 0], sel[:, 1], ALU.add))
                dve.wait_ge(slots_mm, 1)
                link(d.tensor_scalar(slot[:], ps[1][:, 0:NT * E].rearrange("p (t e) -> p t e", t=NT), 1.0, None, ALU.add))
                link(d.tensor_tensor(slot[:], slot[:], chosen[:], ALU.mult))
                link(d.tensor_scalar(slot[:], slot[:], -1.0, None, ALU.add))

                link(d.tensor_reduce(most[:], ps[1][:, 2 * E:3 * E], AX.X, ALU.max))
                d.tensor_scalar(over[:], most[:], float(P), None, ALU.is_gt).then_inc(over_known, 1)
                dve.wait_ge(over_known, 1)
                with dve.If(dve.value_load(over[0:1, 0:1], min_val=0, max_val=1) > 0):
                    d.memset(o_y[:], 0.0).then_inc(o_y_added, 1)
                    dve.wait_ge(o_y_added, 1)
                    with dve.Fori(0, E) as e:
                        d.memset(o_y[:], 0.0).then_inc(o_picked, 1)
                        for t in range(NT):
                            d.tensor_scalar(o_pick[:, t, :], slot_iota[:], float(P), slot[:, t, bass.ds(e, 1)], ALU.add,
                                            ALU.is_equal).then_inc(o_picked, 1)
                        dve.wait_ge(o_gathered, e + 1)
                        d.tensor_copy(o_pickT[:].rearrange("p t s -> p (t s)"), ps[2][:, 0:T]).then_inc(o_copied, 1)
                        d.tensor_copy(c_slot[:], ps[2][:, T:T + 1]).then_inc(o_copied, 1)
                        for h in range(2):
                            d.tensor_copy(o_xg[:, 4 * h:4 * h + 4, :].rearrange("p k s -> p (k s)"), ps[6 + h][:]).then_inc(o_copied, 1)
                        with dve.Fori(0, NB) as b:
                            dve.wait_ge(o_silu, e * NB + b + 1)
                            d.tensor_tensor(o_hid[:], o_sg[:], ps[0][:, FB:2 * FB], ALU.mult).then_inc(o_hid_ready, 1)
                            dve.wait_ge(o_hid_turned, e * NB + b + 1)
                            d.tensor_copy(o_hidT[:].rearrange("p j s -> p (j s)"), ps[2][:, 0:T]).then_inc(o_hidT_ready, 1)
                            dve.wait_ge(o_down_mm, e * NB + b + 1)
                            dve.wait_ge(o_picked, e * 3 + 3)
                            d.tensor_tensor(o_y[:, 0:CW], o_y[:, 0:CW], ps[4][:], ALU.add).then_inc(o_y_ready, 1)
                            d.tensor_tensor(o_y[:, CW:], o_y[:, CW:], ps[5][:], ALU.add).then_inc(o_y_added, 1)
                            dve.wait_ge(o_y_added, e * NB + b + 2)
                            dve.wait_ge(o_y_ready, e * (NB + 1) + b + 1)
                        dve.wait_ge(o_copied, e * 4 + 4)
                        d.tensor_scalar(o_y[:], o_y[:], c_slot[:, 0:1], None, ALU.mult).then_inc(o_y_ready, 1)
                        for q in range(4):
                            dve.wait_ge(o_back, e * 4 + q + 1)
                            xs = x[:, q // 2, (q % 2) * CW:(q % 2 + 1) * CW]
                            d.tensor_tensor(xs, xs, ps[6 + q % 2][:], ALU.add).then_inc(o_added, 1)
                        dve.wait_ge(o_added, e * 4 + 4)
                    dve.wait_ge(o_added, 4 * E)

                def pick_tokens(e, o):
                    for t in range(NT):
                        d.tensor_scalar(pick[:, t, :], slot_iota[:], slot[:, t, bass.ds(e + o, 1)], None, ALU.is_equal).then_inc(e_pick, 1)

                def gathered_lo(e, o):
                    for b in range(2):
                        dve.wait_ge(e_xg_hi, e * 2 + (2 * o + b + 1))
                        d.tensor_tensor(xgl[:, 4 * b:4 * b + 4, :].rearrange("p k s -> p (k s)"), ps[6 + b][:],
                                        xgh[:, 4 * b:4 * b + 4, :].rearrange("p k s -> p (k s)").bitcast(F32),
                                        ALU.subtract).then_inc(e_xg_lo, 1)

                def y_lo(e):
                    for b in range(2):
                        dve.wait_ge(e_y_hi, e * 2 + (b + 1))
                        d.scalar_tensor_tensor(out=yl[:, b * CW:(b + 1) * CW], in0=ps[4 + b][:], scalar=c_slot[:, 0:1],
                                               in1=yh[:, b * CW:(b + 1) * CW].bitcast(F32), op0=ALU.mult, op1=ALU.subtract).then_inc(e_y_lo, 1)

                def add_back(e, t):
                    for h in range(2):
                        dve.wait_ge(e_back, e * 4 + (2 * t + h + 1))
                        xs = x[:, t, h * CW:(h + 1) * CW]
                        d.tensor_tensor(xs, xs, ps[6 + h][:], ALU.add).then_inc(e_added, 1)

                def blocks(e, o, span, more):
                    def split_e(end):
                        while lo_next[0] < end + o * FU:
                            j = lo_next[0]
                            s = j % SLOTS
                            dve.wait_ge(hi_ready, e * FU + (U_MOE + j + 1))
                            d.tensor_tensor(wlo[:, s, :], raw[:, s, :], whi[:, (U_MOE + j) % HIS, :].bitcast(F32),
                                            ALU.subtract).then_inc(lo_ready, 1)
                            lo_next[0] += 1

                    for b in span:
                        if b < NB:
                            split_e(gu_pos[b] + 4)
                            dve.wait_ge(e_silu, e * NB + (o * NB + b + 1))
                            d.tensor_tensor(hid[:, b % 2, 0, :], sg[:, b % 2, :], ps[b % 2][:, FB:2 * FB], ALU.mult).then_inc(e_hid, 1)
                        if 1 <= b <= NB:
                            dve.wait_ge(e_hidT_hi, e * NB + (o * NB + b))
                            d.tensor_tensor(hidTl[:, (b - 1) % 2, :, 0:P], ps[2][:, 0:2 * P].rearrange("p (j t) -> p j t", j=2),
                                            hidTh[:, (b - 1) % 2, :, 0:P].bitcast(F32), ALU.subtract).then_inc(e_hidT_lo, 1)
                        if o and b in (1, 2):
                            add_back(e, b - 1)
                        if b == SPLIT_AT - 1:
                            dve.wait_ge(e_pickT, e + (o + 1))
                            d.tensor_copy(c_slot[:], ps[3][:, T:T + 1]).then_inc(e_pickT_c, 1)
                        if b == PICK_AT and more:
                            pick_tokens(e, o + 1)
                        if b == NB and more:
                            gathered_lo(e, o + 1)
                        if b >= NB:
                            split_e(down_pos[b - 2] + 3)

                pick_tokens(0, 0)
                gathered_lo(0, 0)
                lo_next[0] = HIS
                blocks(0, 0, range(SPLIT_AT), True)
                start = lo_next[0]
                with dve.Fori(0, E - 1) as e:
                    lo_next[0] = start
                    blocks(e, 0, range(SPLIT_AT, NB + 2), True)
                    y_lo(e)
                    blocks(e, 1, range(SPLIT_AT), True)
                assert lo_next[0] == start + FU
                lo_next[0] = start
                blocks(E - 1, 0, range(SPLIT_AT, NB + 2), False)
                y_lo(E - 1)
                for t in range(NT):
                    add_back(E - 1, t)
                lo_next[0] += U_MOE + (E - 1) * FU
                dve.wait_ge(e_added, 4 * E)
                d.tensor_copy(rstd[:], rstd[:]).then_inc(x_ready, 1)

            experts()
            ple(1, XR_PLE1, U_PLE1, 5 * KD, 4)
            normalise(XR_FINAL)

        @block.tensor
        def _(pe):
            m = nc.tensor

            def mm3(o, sh, sl, mh, ml, start, stop, **kw):
                m.matmul(o, sh, mh, start=start, stop=False, **kw)
                m.matmul(o, sl, mh, start=False, stop=False, **kw)
                return m.matmul(o, sh, ml, start=False, stop=stop, **kw)

            def hi(u):
                return whi[:, u % HIS, :]

            def lo(u):
                return wlo[:, slot_of(u), :]

            def turn(r):
                pe.wait_ge(xn_ready, 2 * r + 2)
                for kp in range(KD // 2):
                    for k in (0, 1):
                        for t in range(NT):
                            kk = 2 * kp + k
                            ins = m.transpose(ps[4 + kp][:, k * T + t * P:k * T + (t + 1) * P], xn[:, t, kk * P:(kk + 1) * P], ident[:])
                    ins.then_inc(turned, 1)

            def h_is(nth, k):
                pe.wait_ge(h_ready, (KD // 2) * nth + k // 2 + 1)

            def tokens_out(u0, banks, nth, first):
                for hf in range(2):
                    pe.wait_ge(lo_ready, u0 + hf + 1)
                    for t in range(NT):
                        for kk in range(4):
                            k = 4 * hf + kk
                            if first and t == 0:
                                h_is(nth, k)
                            ins = mm3(ps[banks[t]][:], hTh[:, k, t * P:(t + 1) * P], hTl[:, k, t * P:(t + 1) * P],
                                      hi(u0 + hf)[:, kk * CW:(kk + 1) * CW], lo(u0 + hf)[:, kk * CW:(kk + 1) * CW],
                                      start=k == 0, stop=k == 7)
                    ins.then_inc(unit_used, 1)

            def features_out(u0, hf, banks, nth, first, cgs=range(4)):
                if 0 in cgs:
                    pe.wait_ge(lo_ready, u0 + hf + 1)
                for cg in cgs:
                    for kk in range(4):
                        k = 4 * hf + kk
                        if first and cg == 0:
                            h_is(nth, k)
                        c0 = kk * CW + cg * P
                        ins = mm3(ps[banks[cg // 2]][:, (cg % 2) * T:(cg % 2 + 1) * T], hi(u0 + hf)[:, c0:c0 + P],
                                  lo(u0 + hf)[:, c0:c0 + P], hTh[:, k, :], hTl[:, k, :],
                                  start=k == 0 and cg % 2 == 0, stop=k == 7, skip_group_check=True)
                if 3 in cgs:
                    ins.then_inc(unit_used, 1)

            def rows_out(u, sh, sl, b0, first, last):
                pe.wait_ge(lo_ready, u + 1)
                for kk in range(2):
                    for t in range(NT):
                        for h in range(2):
                            w0 = kk * D + h * CW
                            ins = mm3(ps[b0 + 2 * t + h][:], sh(kk, t), sl(kk, t), hi(u)[:, w0:w0 + CW], lo(u)[:, w0:w0 + CW],
                                      start=first and kk == 0, stop=last and kk == 1)
                ins.then_inc(unit_used, 1)

            pe.wait_ge(consts_ready, 1)
            pe.wait_ge(rows_in, 16 * 13)
            na = (CONV + 3) * KI
            m.transpose(ps[0][:, 0:na], rows_a[0:na, :], ident[0:na, 0:na]).then_inc(prep_turned, 1)
            m.transpose(ps[1][:, 0:6 * KD], rows_b[0:6 * KD, :], ident[0:6 * KD, 0:6 * KD]).then_inc(prep_turned, 1)
            for b in range(2):
                for g in range(4):
                    ins = m.transpose(ps[2 + b][:, g * P:(g + 1) * P], w_s[:, 4 * b + g, :], ident[:])
                ins.then_inc(prep_turned, 1)

            turn(XR_GMLP)
            pe.wait_ge(prep_copied, 3)
            pe.wait_ge(gains_copied, 1)
            for i in range(4):
                if i >= 2:
                    pe.wait_ge(v_gelu, NT * (i - 1))
                tokens_out(U_GIN + 2 * i, (2 * (i % 2), 2 * (i % 2) + 1), 0, i == 0)
            for i in range(4):
                if i < 2:
                    pe.wait_ge(v_gelu, NT * (i + 3))
                else:
                    pe.wait_ge(u_gelu, 2 * (i - 1))
                for hf in range(2):
                    features_out(U_GIN + 8 + 2 * i, hf, (2 * (i % 2), 2 * (i % 2) + 1), 0, False)

            def mix(g):
                if g >= 4:
                    pe.wait_ge(gated_lo, g - 3)
                pe.wait_ge(v_ready, NT)
                for c in range(2):
                    for n in range(NT):
                        cc = 2 * g + c
                        ins = m.matmul(ps[4 + g % 4][:, (c * NT + n) * P:(c * NT + n + 1) * P], v[:, n, cc * P:(cc + 1) * P],
                                       w_sT[:, g, :], start=True, stop=True)
                ins.then_inc(mixed, 1)

            for g in range(4):
                mix(g)
            pe.wait_ge(u_gelu, 8)
            for g in range(G):
                pe.wait_ge(gated_lo, g + 1)
                rows_out(U_GOUT + g, lambda kk, t: ghi[:, t, 2 * g + kk, :], lambda kk, t: glo[:, 2 * g + kk, t * P:(t + 1) * P],
                         0, g == 0, g == G - 1)
                if g + 4 < G:
                    mix(g + 4)

            def dense_ffn():
                turn(XR_FFN)
                for b in range(NB + 2):
                    if b < NB:
                        if b:
                            pe.wait_ge(hid_ready, NT * b)
                        for hf in range(2):
                            u = U_FFN + gu_pos[b] + hf
                            pe.wait_ge(lo_ready, u + 1)
                            for t in range(NT):
                                for kk in range(4):
                                    k = 4 * hf + kk
                                    if b == 0 and t == 0:
                                        h_is(1, k)
                                    ins = mm3(ps[t][:], hTh[:, k, t * P:(t + 1) * P], hTl[:, k, t * P:(t + 1) * P],
                                              hi(u)[:, kk * CW:(kk + 1) * CW], lo(u)[:, kk * CW:(kk + 1) * CW],
                                              start=k == 0, stop=k == 7)
                            ins.then_inc(unit_used, 1)
                    if 1 <= b <= NB:
                        pe.wait_ge(hid_ready, NT * b)
                        if b >= 2:
                            pe.wait_ge(hidT_lo, b - 1)
                        for j in range(2):
                            for t in range(NT):
                                ins = m.transpose(ps[2][:, j * T + t * P:j * T + (t + 1) * P],
                                                  hid[:, (b - 1) % 2, t, j * P:(j + 1) * P], ident[:])
                        ins.then_inc(hid_turned, 1)
                    if b >= 2:
                        pe.wait_ge(hidT_lo, b - 1)
                        rows_out(U_FFN + down_pos[b - 2], lambda kk, t: hidTh[:, b % 2, kk, t * P:(t + 1) * P],
                                 lambda kk, t: hidTl[:, b % 2, kk, t * P:(t + 1) * P], 4, b == 2, b == NB + 1)

            dense_ffn()

            def ple(l, r, base_unit, nth):
                pe.wait_ge(p_in[l], 16)
                if l == 0:
                    pe.wait_ge(hidT_lo, NB)
                for k in range(KP):
                    for t in range(NT):
                        ins = m.transpose(ps[3][:, k * T + t * P:k * T + (t + 1) * P], p_tok[:, t, k * P:(k + 1) * P], ident[:])
                ins.then_inc(p_turned, 1)
                pe.wait_ge(p_ready, l + 1)
                rows_out(base_unit, lambda kk, t: pTh[:, kk, t * P:(t + 1) * P], lambda kk, t: pTl[:, kk, t * P:(t + 1) * P],
                         0, True, True)
                turn(r)
                for i in range(KD // 2):
                    pe.wait_ge(h_ready, (KD // 2) * (nth + 1))
                    rows_out(base_unit + 1 + i, lambda kk, t: hTh[:, 2 * i + kk, t * P:(t + 1) * P],
                             lambda kk, t: hTl[:, 2 * i + kk, t * P:(t + 1) * P], 4, i == 0, i == KD // 2 - 1)

            ple(0, XR_PLE0, U_PLE0, 2)

            def mlstm():
                turn(XR_MLSTM)

                def project(i):
                    pe.wait_ge(bd_ready, i + 1)
                    pe.wait_ge(xc_ready, i + 1)
                    for pr in range(2):
                        n0 = (2 * i + pr) * 4
                        for j in range(4):
                            item = n0 + j
                            if item >= 3:
                                prev = item - 3
                                pq, pj = prev // 4, prev % 4
                                if pj < 2:
                                    pe.wait_ge(qk_copied, 2 * pq + pj + 1)
                                else:
                                    pe.wait_ge(v_copied, 2 * pq + pj - 1)
                            bank = ps[4 + item % 3]
                            for k in range(2):
                                cc = 2 * pr + k
                                if j < 2:
                                    ins = m.matmul(bank[:, k * T:(k + 1) * T], blockdiag[:, j, cc, :], xc[:, 4 * i + cc, :], start=True, stop=True)
                                elif j == 2:
                                    ins = m.matmul(bank[:, k * T:(k + 1) * T], blockdiag[:, 2, cc, :], xpad[:, cc, CONV - 1:], start=True, stop=True)
                                else:
                                    for t in range(NT):
                                        ins = m.matmul(bank[:, t * 2 * P + k * P:t * 2 * P + (k + 1) * P],
                                                       xpad[:, cc, CONV - 1 + t * P:CONV - 1 + (t + 1) * P],
                                                       blockdiag[:, 2, cc, :], start=True, stop=True)
                            ins.then_inc(qkv_mm, 1)
                        pe.wait_ge(qk_copied, 2 * (2 * i + pr) + 2)
                        pe.wait_ge(v_copied, 2 * (2 * i + pr) + 1)
                        for k in range(2):
                            c = 4 * i + 2 * pr + k
                            for j, src in enumerate((qT[:, c, :], kT[:, c, :], vT[:, k, :])):
                                for t in range(NT):
                                    ins = m.matmul(ps[7][:, t * 2 * H:(t + 1) * 2 * H], src[:, t * P:(t + 1) * P],
                                                   w_gate[:, j * KI + c, :], start=c == 0 and j == 0 and t == 0, stop=False,
                                                   skip_group_check=True)
                        if pr == 1:
                            ins.then_inc(bd_used, 1)

                for i in range(4):
                    if i >= 2:
                        pe.wait_ge(xm_copied, i - 1)
                    for hf in range(2):
                        features_out(U_MIN + 2 * i, hf, (2 * (i % 2), 2 * (i % 2) + 1), 3, i == 0)
                    if i:
                        project(i - 1)
                project(3)
                for t in range(NT):
                    ins = m.matmul(ps[7][:, t * 2 * H:(t + 1) * 2 * H], ones[0:1, :], b_gate[0:1, :], start=False, stop=t == NT - 1,
                                   skip_group_check=True)
                ins.then_inc(gates_mm, 1)

                def z_block(i, hf, cgs=range(4)):
                    if i:
                        pe.wait_ge(z_exp, 2 * i)
                    features_out(U_MIN + 8 + 2 * i, hf, (0, 1), 3, False, cgs)

                pe.wait_ge(xm_copied, 4)
                z_block(0, 0)
                pe.wait_ge(logf_ready, 1)
                m.matmul(ps[7][:, 64:64 + H], tri_incl[:], logf[:, 0, :], start=True, stop=True)
                m.matmul(ps[7][:, 64 + H:64 + 2 * H], ones[:], logf[:, 0, :], start=True, stop=False)
                m.matmul(ps[7][:, 64 + H:64 + 2 * H], tri_incl[:], logf[:, 1, :], start=False, stop=True).then_inc(cums_mm, 1)
                z_block(0, 1, range(0, 2))
                pe.wait_ge(a_ready, 1)
                for t in range(NT):
                    ins = m.transpose(ps[7][0:H, 256 + t * P:256 + (t + 1) * P], a_tok[:, t, :], ident[:])
                ins.then_inc(a_turned, 1)
                z_block(0, 1, range(2, 4))
                pe.wait_ge(m_ready, 1)
                for t in range(NT):
                    ins = m.transpose(ps[7][:, 96 + t * H:96 + (t + 1) * H], scan[0][:, P + t * P:P + (t + 1) * P], ident[0:H, 0:H])
                ins.then_inc(m_turned, 1)

                def scores(h):
                    if h >= 2:
                        pe.wait_ge(p_weights, h - 1)
                    if h == 0:
                        pe.wait_ge(v_copied, 16)
                        pe.wait_ge(qk_copied, 16)
                    if h == 1:
                        pe.wait_ge(m_tok_ready, 1)
                    sb = ps[4 + h % 2]
                    for k in range(2):
                        m.matmul(sb[:, 0:T], kT[:, 2 * h + k, 0:P], qT[:, 2 * h + k, :], start=k == 0, stop=k == 1)
                    for k in range(2):
                        m.matmul(sb[:, T:T + P], kT[:, 2 * h + k, P:T], qT[:, 2 * h + k, P:T], start=k == 0, stop=k == 1)
                    m.matmul(ps[6 + h % 2][:, 0:T], ident[0:H, h:h + 1].to_broadcast([H, P]), scan[0][:, P:],
                             start=True, stop=True).then_inc(scores_mm, 1)

                def values(h):
                    pe.wait_ge(p_weights, h + 1)
                    if h:
                        pe.wait_ge(num_copied, h)
                    vh = v_m[:, :, h * DH:(h + 1) * DH]
                    pw = pT[:, h % 2, :]
                    for t, srcs in ((0, ((0, 0),)), (1, ((0, P), (1, 2 * P)))):
                        for n, (s, c0) in enumerate(srcs):
                            m.matmul(ps[2][:, t * DH:(t + 1) * DH], pw[:, c0:c0 + P], vh[:, s, :], start=n == 0, stop=n == len(srcs) - 1)
                    for t, srcs in ((0, ((0, 0),)), (1, ((0, P), (1, 2 * P)))):
                        for n, (s, c0) in enumerate(srcs):
                            ins = m.matmul(ps[3][:, t * H + h:t * H + h + 1], pw[:, c0:c0 + P], ones[:, 0:1], start=n == 0, stop=n == len(srcs) - 1)
                    ins.then_inc(num_mm, 1)

                for i in range(4):
                    for h in (2 * i, 2 * i + 1):
                        scores(h)
                        if h:
                            values(h - 1)
                    if i < 3:
                        for hf in range(2):
                            z_block(i + 1, hf)
                values(H - 1)
                m.matmul(ps[3][:, 32:33], ones[:], ones[:, 0:1], start=True, stop=True).then_inc(num_mm, 1)

                def turn_hn(g):
                    pe.wait_ge(hn_ready, g + 1)
                    if g >= 4:
                        pe.wait_ge(mixed_lo, g - 3)
                    for k in range(2):
                        for t in range(NT):
                            ins = m.transpose(ps[4 + g % 4][:, k * T + t * P:k * T + (t + 1) * P], num[:, g, t, k * P:(k + 1) * P], ident[:])
                    ins.then_inc(hn_turned, 1)

                for g in range(4):
                    turn_hn(g)
                pe.wait_ge(z_exp, 8)
                for g in range(H):
                    pe.wait_ge(mixed_lo, g + 1)
                    rows_out(U_MOUT + g, lambda kk, t: ohi[:, 2 * g + kk, t * P:(t + 1) * P],
                             lambda kk, t: olo[:, 2 * g + kk, t * P:(t + 1) * P], 0, g == 0, g == H - 1)
                    if g + 4 < H:
                        turn_hn(g + 4)

            mlstm()

            def experts():
                turn(XR_MOE)
                for k in range(KD):
                    pe.wait_ge(hT32_ready, k // 2 + 1)
                    for t in range(NT):
                        ins = m.matmul(ps[0][:, t * E:(t + 1) * E], hT32[:, k, t * P:(t + 1) * P], router[:, k, :],
                                       start=k == 0 and t == 0, stop=k == KD - 1, skip_group_check=True)
                ins.then_inc(logits_mm, 1)
                pe.wait_ge(chosen_ready, 1)
                m.matmul(ps[1][:, 0:E], tri_strict[:], chosen[:, 0, :], start=True, stop=True)
                m.matmul(ps[1][:, E:2 * E], ones[:], chosen[:, 0, :], start=True, stop=False)
                m.matmul(ps[1][:, E:2 * E], tri_strict[:], chosen[:, 1, :], start=False, stop=True)
                for t in range(NT):
                    ins = m.matmul(ps[1][:, 2 * E:3 * E], ones[:], chosen[:, t, :], start=t == 0, stop=t == NT - 1)
                ins.then_inc(slots_mm, 1)
                pe.wait_ge(hl_ready, 1)
                pe.wait_ge(prob_exp, 1)
                pe.wait_ge(over_known, 1)
                with pe.If(pe.value_load(over[0:1, 0:1], min_val=0, max_val=1) > 0):
                    with pe.Fori(0, E) as e:
                        pe.wait_ge(o_picked, e * 3 + 3)
                        for t in range(NT):
                            m.transpose(ps[2][:, t * P:(t + 1) * P], o_pick[:, t, :], ident[:])
                        for t in range(NT):
                            m.matmul(ps[2][:, T:T + 1], o_pick[:, t, :], comb[:, t, bass.ds(e, 1)], start=t == 0, stop=t == NT - 1)
                        for k in range(KD):
                            for t in range(NT):
                                ins = m.matmul(ps[6 + k // 4][:, (k % 4) * P:(k % 4 + 1) * P], xn[:, t, k * P:(k + 1) * P],
                                               o_pick[:, t, :], start=t == 0, stop=t == NT - 1)
                        ins.then_inc(o_gathered, 1)
                        with pe.Fori(0, NB) as b:
                            pe.wait_ge(o_copied, e * 4 + 4)
                            pe.wait_ge(o_landed, (e * NB + b) * 48 + 48)
                            for j, w in enumerate((o_gate, o_up)):
                                for k in range(KD):
                                    ins = m.matmul(ps[0][:, j * FB:(j + 1) * FB], o_xg[:, k, :], w[:, k, :], start=k == 0, stop=k == KD - 1)
                            ins.then_inc(o_gu_mm, 1)
                            pe.wait_ge(o_hid_ready, e * NB + b + 1)
                            for j in range(2):
                                ins = m.transpose(ps[2][:, j * P:(j + 1) * P], o_hid[:, j * P:(j + 1) * P], ident[:])
                            ins.then_inc(o_hid_turned, 1)
                            pe.wait_ge(o_hidT_ready, e * NB + b + 1)
                            for h in range(2):
                                for j in range(2):
                                    ins = m.matmul(ps[4 + h][:], o_hidT[:, j, :], o_down[:, j, h * CW:(h + 1) * CW], start=j == 0, stop=j == 1)
                            ins.then_inc(o_down_mm, 1)
                            pe.wait_ge(o_y_added, e * NB + b + 2)
                        pe.wait_ge(o_y_ready, e * (NB + 1) + (NB + 1))
                        for q in range(4):
                            t, h = q // 2, q % 2
                            if q >= 2:
                                pe.wait_ge(o_added, e * 4 + q - 1)
                            m.matmul(ps[6 + h][:], o_pickT[:, t, :], o_y[:, h * CW:(h + 1) * CW], start=True, stop=True).then_inc(o_back, 1)
                        pe.wait_ge(o_added, e * 4 + 4)
                    pe.wait_ge(o_added, 4 * E)

                def gather(e, o):
                    pe.wait_ge(e_pick, e * NT + (o * NT + NT))
                    for k in range(KD):
                        for t in range(NT):
                            m.matmul(ps[6 + k // 4][:, (k % 4) * P:(k % 4 + 1) * P], hh[:, t, k * P:(k + 1) * P], pick[:, t, :],
                                     start=t == 0, stop=False)
                            ins = m.matmul(ps[6 + k // 4][:, (k % 4) * P:(k % 4 + 1) * P], hl[:, t, k * P:(k + 1) * P], pick[:, t, :],
                                           start=False, stop=t == NT - 1)
                        if k % 4 == 3:
                            ins.then_inc(e_gathered, 1)

                def turn_pick(e, o):
                    for t in range(NT):
                        m.transpose(ps[3][:, t * P:(t + 1) * P], pick[:, t, :].bitcast(F32), ident[:])
                    for t in range(NT):
                        ins = m.matmul(ps[3][:, T:T + 1], pick[:, t, :].bitcast(F32), comb[:, t, bass.ds(e + o, 1)], start=t == 0, stop=t == NT - 1)
                    ins.then_inc(e_pickT_mm, 1)

                def back(e, t):
                    if t == 0:
                        pe.wait_ge(e_y_lo, e * 2 + 2)
                        pe.wait_ge(e_pickT, e + 1)
                    else:
                        pe.wait_ge(e_added, e * 4 + 2)
                    for h in range(2):
                        m.matmul(ps[6 + h][:], pickT[:, t, :], yh[:, h * CW:(h + 1) * CW], start=True, stop=False)
                        m.matmul(ps[6 + h][:], pickT[:, t, :], yl[:, h * CW:(h + 1) * CW], start=False, stop=True).then_inc(e_back, 1)

                def blocks(e, o, span, more):
                    def unit(j):
                        pe.wait_ge(lo_ready, e * FU + (o * FU + U_MOE + j + 1))
                        return whi[:, (U_MOE + j) % HIS, :], wlo[:, j % SLOTS, :]

                    for b in span:
                        if b < NB:
                            for hf in range(2):
                                wh, wl = unit(gu_pos[b] + hf)
                                for kk in range(4):
                                    k = 4 * hf + kk
                                    if b == 0 and k % 4 == 0:
                                        pe.wait_ge(e_xg_lo, e * 2 + (o * 2 + k // 4 + 1))
                                    ins = mm3(ps[b % 2][:], xgh[:, k, :], xgl[:, k, :], wh[:, kk * CW:(kk + 1) * CW],
                                              wl[:, kk * CW:(kk + 1) * CW], start=k == 0, stop=k == 7)
                                ins.then_inc(unit_used, 1)
                        if 1 <= b <= NB:
                            pe.wait_ge(e_hid, e * NB + (o * NB + b))
                            if b > 1:
                                pe.wait_ge(e_hidT_lo, e * NB + (o * NB + b - 1))
                            for j in range(2):
                                ins = m.transpose(ps[2][:, j * P:(j + 1) * P], hid[:, (b - 1) % 2, 0, j * P:(j + 1) * P], ident[:])
                            ins.then_inc(e_hid_turned, 1)
                        if o and b == 1:
                            back(e, 0)
                        if b >= 2:
                            wh, wl = unit(down_pos[b - 2])
                            pe.wait_ge(e_hidT_lo, e * NB + (o * NB + b - 1))
                            for kk in range(2):
                                for h in range(2):
                                    w0 = kk * D + h * CW
                                    ins = mm3(ps[4 + h][:], hidTh[:, b % 2, kk, 0:P], hidTl[:, b % 2, kk, 0:P],
                                              wh[:, w0:w0 + CW], wl[:, w0:w0 + CW],
                                              start=b == 2 and kk == 0, stop=b == NB + 1 and kk == 1)
                            ins.then_inc(unit_used, 1)
                        if o and b == 2:
                            back(e, 1)
                        if b == SPLIT_AT - 1:
                            if o:
                                pe.wait_ge(e_added, e * 4 + 4)
                            turn_pick(e, o)
                        if b == GATHER_AT and more:
                            gather(e, o + 1)

                gather(0, 0)
                blocks(0, 0, range(SPLIT_AT), True)
                with pe.Fori(0, E - 1) as e:
                    blocks(e, 0, range(SPLIT_AT, NB + 2), True)
                    blocks(e, 1, range(SPLIT_AT), True)
                blocks(E - 1, 0, range(SPLIT_AT, NB + 2), False)
                for t in range(NT):
                    back(E - 1, t)
                pe.wait_ge(e_pickT_c, E)
                pe.wait_ge(e_added, 4 * E)

            experts()
            ple(1, XR_PLE1, U_PLE1, 4)


def add_to_x_banks(d, x, ps, b0, cw, nt):
    for t in range(nt):
        for h in range(2):
            xs = x[:, t, h * cw:(h + 1) * cw]
            ins = d.tensor_tensor(xs, xs, ps[b0 + 2 * t + h][:], ALU.add)
    return ins


_INS = ["x", "p", "norm_mix", "norm_ffn", "norm_ple", "norm_final", "ga_w_in", "ga_ln_g", "ga_ln_b", "ga_w_s", "ga_b_s",
        "ga_w_out", "mb_w_in", "mb_conv_w", "mb_conv_b", "mb_wq", "mb_wk", "mb_wv", "mb_w_gate", "mb_b_gate", "mb_norm_g",
        "mb_skip", "mb_w_out", "fd_w_gate", "fd_w_up", "fd_w_down", "fe_router", "fe_w_gate", "fe_w_up", "fe_w_down",
        "ple_w_proj", "ple_w_gate"]


def kernel(**inputs):
    import numpy as np
    import concourse.bacc as bacc
    from concourse.bass_utils import run_bass_kernel_spmd

    nc = bacc.Bacc("TRN2", target_bir_lowering=False, num_devices=1)
    arrays = {f"in_{name}": np.ascontiguousarray(inputs[name]) for name in _INS}
    aps = {name: nc.dram_tensor(f"in_{name}", arrays[f"in_{name}"].shape, mybir.dt.from_np(arrays[f"in_{name}"].dtype),
                                kind="ExternalInput").ap() for name in _INS}
    shape = inputs["x"].shape
    out = nc.dram_tensor("out_0", shape, F32, kind="ExternalOutput").ap()
    build(nc, aps, out)
    r = run_bass_kernel_spmd(nc, [arrays], core_ids=[0])
    return r.results[0]["out_0"]
```

```python
from contextlib import ExitStack

import concourse.bass as bass
from concourse import mybir

F32 = mybir.dt.float32
F32R = mybir.dt.float32r
I32 = mybir.dt.int32
ALU = mybir.AluOpType
ACT = mybir.ActivationFunctionType
AX = mybir.AxisListType

P = 128
EPS = 1e-6
BIG = 3.0e38
RSQRT_SEED = 1597463007.0


def stream_positions(n_blocks):
    gate_up, down, order = {}, {}, []
    for b in range(n_blocks + 2):
        if b < n_blocks:
            gate_up[b] = len(order)
            order += [("gu", b, 0), ("gu", b, 1)]
        if b >= 2:
            down[b - 2] = len(order)
            order.append(("down", b - 2, 0))
    return gate_up, down, order


def build(nc, A, out):
    _, T, D = A["x"].shape
    NT = T // P
    KD = D // P
    PLE = A["p"].shape[-1]
    KP = PLE // P
    G = A["ga_w_s"].shape[1]
    GD = A["ga_ln_g"].shape[1]
    KG = GD // P
    H = A["mb_w_gate"].shape[-1] // 2
    DI = A["mb_w_in"].shape[-1] // 2
    KI = DI // P
    DH = DI // H
    CONV = A["mb_conv_w"].shape[1]
    NBLK = A["mb_wq"].shape[1]
    QB = A["mb_wq"].shape[2]
    E = A["fe_router"].shape[-1]
    F = A["fd_w_gate"].shape[-1]
    FB = 256
    NB = F // FB
    CW = 512
    assert NT == 2 and KD == 8 and KP == 2 and KG == 16 and KI == 16 and H == G == E == 8 and DH == 256
    assert NB * FB == F and QB == 4 and NBLK == 32 * KI and CONV == 4

    gu_pos, down_pos, ffn_order = stream_positions(NB)
    FU = len(ffn_order)

    units = []
    in_order = [4, 5, 6, 7, 0, 1, 2, 3]
    U_GIN = len(units)
    units += [("in", (A["ga_w_in"][0],), cb, h) for cb in in_order for h in range(2)]
    U_GOUT = len(units)
    units += [("out", (A["ga_w_out"][0],), i, 0) for i in range(KG // 2)]
    U_FFN = len(units)
    dense = (A["fd_w_gate"][0], A["fd_w_up"][0], A["fd_w_down"][0])
    units += [(kind, dense, b, h) for kind, b, h in ffn_order]
    U_PLE0 = len(units)
    units += [("out", (A["ple_w_proj"][0],), 0, 0)] + [("out", (A["ple_w_gate"][0],), i, 0) for i in range(KD // 2)]
    U_MIN = len(units)
    units += [("in", (A["mb_w_in"][0],), cb, h) for cb in range(8) for h in range(2)]
    U_MOUT = len(units)
    units += [("out", (A["mb_w_out"][0],), i, 0) for i in range(KI // 2)]
    U_MOE = len(units)
    U_PLE1 = U_MOE + E * FU
    ple1_units = [("out", (A["ple_w_proj"][1],), 0, 0)] + [("out", (A["ple_w_gate"][1],), i, 0) for i in range(KD // 2)]

    SLOTS = 11
    LENT = 4
    EARLY = SLOTS - LENT
    HIS = 3
    HALVES = (slice(0, 1024), slice(1024, 2048))
    assert FU % SLOTS == 0 and FU % HIS == 0

    def slot_of(u):
        return u % EARLY if u < U_MOE else (u - U_MOE) % SLOTS

    early_uses = [len([u for u in range(U_MOE) if u % EARLY == s]) if s < EARLY else 0 for s in range(SLOTS)]

    def uses_before(u):
        if u < U_MOE:
            return u // EARLY
        return early_uses[slot_of(u)] + (u - U_MOE) // SLOTS

    with ExitStack() as ctx:
        base = (nc.sbuf_base + 31) // 32 * 32
        UNIT = 2048
        KB = 1024
        O_RING = 0
        O_HI = O_RING + SLOTS * 8 * KB
        O_X = O_HI + HIS * 8 * KB
        O_XN = O_X + 8 * KB
        O_HTH = O_XN + 8 * KB
        O_HTL = O_HTH + 8 * KB
        O_C = O_HTL + 8 * KB
        O_LENT = O_RING + EARLY * 8 * KB
        cursor = [O_C]

        def at(name, off, shape, dt=F32):
            return nc.alloc_sbuf_tensor_at(name, shape, dt, offset=base + off)

        def const(name, shape, dt=F32):
            n = 1
            for s in shape[1:]:
                n *= s
            t = at(name, cursor[0], shape, dt)
            cursor[0] += (4 * n + 31) // 32 * 32
            return t

        raw = at("raw_weights", O_RING, [P, SLOTS, UNIT])
        wlo = at("weights_lo", O_RING, [P, SLOTS, UNIT], F32R)
        whi = at("weights_hi", O_HI, [P, HIS, UNIT], F32R)
        x = at("x_res", O_X, [P, NT, D])
        xn = at("x_normed", O_XN, [P, NT, D])
        hTh = at("hT_hi", O_HTH, [P, KD, T], F32R)
        hTl = at("hT_lo", O_HTL, [P, KD, T], F32R)

        ident = const("ident", [P, P])
        tri_incl = const("tri_incl", [P, P])
        tri_strict = const("tri_strict", [P, P])
        ones = const("ones", [P, P])
        far = const("masked_far", [P, P])
        slot_iota = const("slot_iota", [P, P])
        earlier = const("earlier_expert", [P, E, E])
        own_block = const("own_block", [P, 32])
        vec_a = const("vec_a", [P, CONV * KI + 3 * KI])
        vec_b = const("vec_b", [P, 6 * KD])
        qkv_w = const("qkv_w", [P, 3, KI, QB])
        w_gate = const("w_gate", [P, 3 * KI, 2 * H])
        router = const("router", [P, KD, E])
        b_gate = const("b_gate", [1, 2 * H])
        ss = const("sum_squares", [P, NT])
        var = const("variance", [P, NT])
        rstd = const("rstd", [P, NT])
        newton = const("newton", [P, NT * H])
        ln_stats = const("ln_stats", [P, NT, 4, 6])
        ln_mv = const("ln_mv", [P, NT, 2])
        gates = const("gates", [P, NT, 2 * H])
        gate_t = const("gate_tmp", [P, NT, H])
        gate_e = const("gate_exp", [P, NT, H])
        logf = const("log_f", [P, NT, H])
        a_tok = const("a_tok", [P, NT, H])
        b_tok = const("b_tok", [P, NT, H])
        emt = const("exp_minus_m", [P, NT, H])
        qn = const("qn", [P, NT, H])
        head_stats = const("head_stats", [P, NT, H, 6])
        head_mv = const("head_mv", [P, NT, H, 2])
        head_r = const("head_r", [P, NT, H])
        head_v = const("head_v", [P, NT, H])
        head_s = const("head_s", [P, NT, H])
        logits = const("logits", [P, NT, E])
        rank = const("rank", [P, NT, E])
        sel = const("sel", [P, 2, NT, E])
        top = const("top", [P, 2, NT])
        prob = const("prob", [P, 2, NT])
        comb = const("combine", [P, NT, E])
        chosen = const("chosen", [P, NT, E])
        picked = const("picked_logits", [P, 2, NT, E])
        slot = const("slot_of_token", [P, NT, E])
        c_slot = const("slot_weight", [P, 1])
        most = const("most_tokens", [P, 1])
        over = const("over_flag", [P, 1], I32)
        O_PH = cursor[0]
        assert base + O_PH + 3 * 16 * KB + 4352 <= nc.sbuf_usable_end, (O_PH, nc.sbuf_usable_end)

        uT = at("uT", O_PH, [P, KG, T])
        glo = at("gated_lo", O_PH, [P, KG, T], F32R)
        rows_a = at("rows_a", O_PH + 44 * KB, [P, P])
        rows_b = at("rows_b", O_PH, [P, P])
        v = at("v_tok", O_PH + 16 * KB, [P, NT, GD])
        ghi = at("gated_hi", O_PH + 16 * KB, [P, NT, KG, P], F32R)
        w_s = at("w_spatial", O_PH + 32 * KB, [P, G, P])
        w_sT = at("w_spatialT", O_PH + 36 * KB, [P, G, P])
        b_s = at("b_spatial", O_PH + 40 * KB, [P, G, P])
        gtmp = at("gmlp_tmp", O_PH + 44 * KB, [P, 2, NT, P])
        ln_g = at("ln_g", O_LENT, [P, GD])
        ln_b = at("ln_b", O_LENT + 8 * KB, [P, GD])
        gprod = at("gmlp_prod", O_XN, [P, 2, 2, NT, P])
        lent_halves = at("xc_and_z", O_LENT, [P, 2, 2, KI // 2, T])

        def xc(c, n=1):
            return lent_halves[:, c // 8, 0, c % 8:c % 8 + n, :]

        def sz(c, n=1):
            return lent_halves[:, c // 8, 1, c % 8:c % 8 + n, :]

        qT = at("qT", O_PH, [P, KI, T])
        num = at("numerator", O_PH, [P, H, NT, DH])
        ohi = at("mixed_hi", O_PH, [P, KI, T], F32R)
        kT = at("kT", O_PH + 16 * KB, [P, KI, T])
        olo = at("mixed_lo", O_PH + 16 * KB, [P, KI, T], F32R)
        v_m = at("v_mlstm", O_PH + 32 * KB, [P, NT, DI])
        xpad = at("xm_padded", O_PH + 48 * KB, [P, 4, CONV - 1 + T])
        blockdiag = at("blockdiag", O_XN, [P, 3, 4, P])
        vT = at("vT", O_XN + 6 * KB, [P, 2, T])
        ROW = P + T
        scan = [at(f"scan_{i}", O_PH + 48 * KB + i * 4 * ROW, [H, ROW]) for i in range(2)]
        arg = at("decay_arg", O_XN, [P, 3 * P])
        wexp = at("decay", O_XN + 1536, [P, 2, 3 * P])
        pT = at("pT_weights", O_XN + 4608, [P, 2, 3 * P])
        otmp = at("out_tmp", O_XN, [P, 2, 2, T])
        sg = at("silu_gate", O_PH, [P, 2, FB])
        hid = at("hidden", O_PH + 2 * KB, [P, 2, NT, FB])
        hidTh = at("hiddenT_hi", O_PH + 6 * KB, [P, 2, 2, T], F32R)
        hidTl = at("hiddenT_lo", O_PH + 10 * KB, [P, 2, 2, T], F32R)
        p_tok = at("p_tok", O_PH + 14 * KB, [P, NT, PLE])
        pTh = at("pT_hi", O_PH + 16 * KB, [P, KP, T], F32R)
        pTl = at("pT_lo", O_PH + 18 * KB, [P, KP, T], F32R)
        psig = at("ple_gate", O_PH + 20 * KB, [P, NT, D])
        hT32 = at("hT_full", O_HTH, [P, KD, T])
        hh = at("h_hi", O_PH + 28 * KB, [P, NT, D], F32R)
        hl = at("h_lo", O_PH + 36 * KB, [P, NT, D], F32R)
        g_row = at("gain_row", O_PH + 44 * KB, [P, D])
        cmp = at("rank_cmp", O_PH + 16 * KB, [P, 2, NT, E, E])
        xgh = at("gathered_hi", O_HTH, [P, KD, P], F32R)
        xgl = at("gathered_lo", O_HTL, [P, KD, P], F32R)
        pick = at("pick", O_PH + 48 * KB, [P, NT, P], F32R)
        pickT = at("pickT", O_PH + 49 * KB, [P, NT, P], F32R)
        yh = at("y_hi", O_PH + 20 * KB, [P, D], F32R)
        yl = at("y_lo", O_PH + 24 * KB, [P, D], F32R)

        o_gate = at("over_gate", O_PH, [P, KD, FB])
        o_up = at("over_up", O_HTL, [P, KD, FB])
        o_down = at("over_down", O_PH + 20 * KB, [P, 2, D])
        o_sg = at("over_silu", O_PH + 8 * KB, [P, FB])
        o_hid = at("over_hidden", O_PH + 9 * KB, [P, FB])
        o_hidT = at("over_hiddenT", O_PH + 10 * KB, [P, 2, P])
        o_y = at("over_y", O_PH + 16 * KB, [P, D])
        o_xg = at("over_gathered", O_HTH, [P, KD, P])
        o_pick = at("over_pick", O_PH + 48 * KB, [P, NT, P])
        o_pickT = at("over_pickT", O_PH + 49 * KB, [P, NT, P])

        ps = [ctx.enter_context(nc.psum_tensor(f"bank{i}", [P, 512], F32)) for i in range(8)]

        def sem(name):
            return ctx.enter_context(nc.semaphore(name))

        landed = [sem(f"landed_{s}") for s in range(SLOTS)]
        hi_ready = sem("hi_ready")
        lo_ready = sem("lo_ready")
        unit_used = sem("unit_used")
        x_in = sem("x_in_tile_0")
        x_in2 = sem("x_in_tile_1")
        sums = sem("sums")
        gain_rows_in = sem("gain_rows_in")
        rows_in = sem("rows_in")
        ident_ready = sem("ident_ready")
        spatial_in = sem("spatial_in")
        ln_in = sem("ln_in")
        mlstm_in = sem("mlstm_in")
        p_in = [sem("p_in_0"), sem("p_in_1")]
        gain_in = sem("gain_in")
        final_in = sem("final_in")
        out_done = sem("out_done")
        pool_step = sem("pool_step")
        dve_step = sem("dve_step")
        act_step = sem("act_step")
        consts_ready = sem("consts_ready")
        prep_turned = sem("prep_turned")
        prep_copied = sem("prep_copied")
        gains_copied = sem("gains_copied")
        x_ready = sem("x_ready")
        squares = sem("squares")
        xn_ready = sem("xn_ready")
        rstd_ready = sem("rstd_ready")
        turned = sem("turned")
        hi_turned = sem("hi_turned")
        h_ready = sem("h_ready")
        v_gelu = sem("v_gelu")
        v_normed = sem("v_normed")
        v_ready = sem("v_ready")
        u_gelu = sem("u_gelu")
        mixed = sem("mixed")
        gated = sem("gated")
        gated_hi = sem("gated_hi")
        gated_lo = sem("gated_lo")
        silu_done = sem("silu_done")
        hid_ready = sem("hid_ready")
        hid_turned = sem("hid_turned")
        hidT_hi = sem("hidT_hi")
        hidT_lo = sem("hidT_lo")
        p_turned = sem("p_turned")
        p_hi = sem("p_hi")
        p_ready = sem("p_ready")
        ple_sig = sem("ple_sig")
        bd_ready = sem("bd_ready")
        xm_copied = sem("xm_copied")
        conv_first = sem("conv_first")
        pad_ready = sem("pad_ready")
        conv_done = sem("conv_done")
        xc_ready = sem("xc_ready")
        qkv_mm = sem("qkv_mm")
        qk_copied = sem("qk_copied")
        v_copied = sem("v_copied")
        bd_used = sem("bd_used")
        gates_mm = sem("gates_mm")
        forget_in = sem("forget_in")
        forget_ln = sem("forget_ln")
        logf_ready = sem("logf_ready")
        cums_mm = sem("cums_mm")
        a_ready = sem("a_ready")
        a_turned = sem("a_turned")
        m_ready = sem("m_ready")
        m_turned = sem("m_turned")
        m_tok_ready = sem("m_tok_ready")
        emt_ready = sem("emt_ready")
        scores_mm = sem("scores_mm")
        arg_ready = sem("arg_ready")
        decay_ready = sem("decay_ready")
        p_weights = sem("p_weights")
        num_mm = sem("num_mm")
        num_copied = sem("num_copied")
        z_copied = sem("z_copied")
        qn_copied = sem("qn_copied")
        skip_ready = sem("skip_ready")
        z_ready = sem("z_ready")
        hn_ready = sem("hn_ready")
        hn_turned = sem("hn_turned")
        mixed_ready = sem("mixed_ready")
        mixed_hi = sem("mixed_hi")
        mixed_lo = sem("mixed_lo")
        h_gained = sem("h_gained")
        hh_ready = sem("hh_ready")
        hl_ready = sem("hl_ready")
        turned32 = sem("turned32")
        hT32_even = sem("hT32_even")
        hT32_odd = sem("hT32_odd")
        comb_ready = sem("comb_ready")
        logits_mm = sem("logits_mm")
        prob_exp = sem("prob_exp")
        chosen_ready = sem("chosen_ready")
        slots_mm = sem("slots_mm")
        slots_ready = sem("slots_ready")
        over_known = sem("over_known")
        o_picked = sem("o_picked")
        o_gathered = sem("o_gathered")
        o_copied = sem("o_copied")
        o_landed = sem("o_landed")
        o_gu_mm = sem("o_gu_mm")
        o_silu = sem("o_silu")
        o_hid_ready = sem("o_hid_ready")
        o_hid_turned = sem("o_hid_turned")
        o_hidT_ready = sem("o_hidT_ready")
        o_down_mm = sem("o_down_mm")
        o_y_added = sem("o_y_added")
        o_y_ready = sem("o_y_ready")
        o_back = sem("o_back")
        o_added = sem("o_added")
        e_pick = sem("e_pick")
        e_gathered = sem("e_gathered")
        e_xg_hi = sem("e_xg_hi")
        e_xg_lo = sem("e_xg_lo")
        e_pickT_mm = sem("e_pickT_mm")
        e_pickT = sem("e_pickT")
        e_pickT_c = sem("e_pickT_c")
        e_silu = sem("e_silu")
        e_hid = sem("e_hid")
        e_hid_turned = sem("e_hid_turned")
        e_hidT_hi = sem("e_hidT_hi")
        e_hidT_lo = sem("e_hidT_lo")
        e_y_hi = sem("e_y_hi")
        e_y_lo = sem("e_y_lo")
        e_back = sem("e_back")
        e_added = sem("e_added")

        block = ctx.enter_context(nc.Block())

        SPLIT_AT, PICK_AT, GATHER_AT = 4, 6, 8
        Z_BANKS = (0, 2, 0, 0)
        XR_GMLP, XR_FFN, XR_PLE0, XR_MLSTM, XR_MOE, XR_PLE1, XR_FINAL = range(7)
        XN_NTH = {XR_GMLP: 0, XR_MLSTM: 1, XR_FINAL: 2}
        RSTD_NTH = {XR_FFN: 0, XR_PLE0: 1, XR_MOE: 2, XR_PLE1: 3}

        def unit_parts(kind, tensors, i, h):
            if kind == "in":
                src = tensors[0][4 * h * P:(4 * h + 4) * P, i * CW:(i + 1) * CW].rearrange("(k p) n -> p k n", p=P)
                return [(lambda r, k=k: r.rearrange("p (k n) -> p k n", k=4)[:, k:k + 2, :], src[:, k:k + 2, :])
                        for k in (0, 2)]
            if kind in ("out", "down"):
                w = tensors[-1]
                src = w[2 * i * P:(2 * i + 2) * P, :].rearrange("(k p) n -> p k n", p=P)
                return [(lambda r, k=k: r.rearrange("p (k n) -> p k n", k=2)[:, k, :], src[:, k, :]) for k in (0, 1)]
            parts = []
            for j in (0, 1):
                src = tensors[j][4 * h * P:(4 * h + 4) * P, i * FB:(i + 1) * FB].rearrange("(k p) n -> p k n", p=P)
                parts.append((lambda r, j=j: r.rearrange("p (k j n) -> p k j n", k=4, j=2)[:, :, j, :], src))
            return parts

        @block.sync
        def _(sp):
            def load(s, unit):
                for dst, src in unit_parts(*unit):
                    sp.dma_start(dst(raw[:, s, :]), src).then_inc(landed[s], 16)

            sp.dma_start(x[:, 0, :], A["x"][0, 0:P, :]).then_inc(x_in, 16)
            sp.dma_start(x[:, 1, :], A["x"][0, P:2 * P, :]).then_inc(x_in2, 16)
            for u in range(U_MOE):
                if u >= EARLY:
                    sp.wait_ge(unit_used, u - EARLY + 1)
                load(slot_of(u), units[u])

            def expert_unit(e, j):
                kind, b, h = ffn_order[j]
                return (kind, (A["fe_w_gate"][0, e], A["fe_w_up"][0, e], A["fe_w_down"][0, e]), b, h)

            for m in range(SLOTS):
                if m < EARLY:
                    sp.wait_ge(unit_used, max(u for u in range(U_MOE) if slot_of(u) == m) + 1)
                else:
                    sp.wait_ge(mixed_ready, H // 2 if m < EARLY + 2 else H)
                load(m, expert_unit(0, m))
            with sp.Fori(0, E - 1) as e:
                for j in range(SLOTS, SLOTS + FU):
                    sp.wait_ge(unit_used, e * FU + (U_MOE + j - SLOTS + 1))
                    load(j % SLOTS, expert_unit(e + 1 if j >= FU else e, j % FU))
            for j in range(SLOTS, FU):
                sp.wait_ge(unit_used, (E - 1) * FU + U_MOE + j - SLOTS + 1)
                load(j % SLOTS, expert_unit(E - 1, j))
            for i, unit in enumerate(ple1_units):
                sp.wait_ge(unit_used, U_PLE1 + i - SLOTS + 1)
                load(slot_of(U_PLE1 + i), unit)
            sp.wait_ge(out_done, 16 * NT)

        @block.gpsimd
        def _(pool):
            n = [0]

            def link(ins):
                n[0] += 1
                ins.then_inc(pool_step, 1)
                pool.wait_ge(pool_step, n[0])

            g = nc.gpsimd
            g.memset(ident[:], 0.0).then_inc(pool_step, 1)
            g.memset(ones[:], 1.0).then_inc(pool_step, 1)
            n[0] += 2
            pool.wait_ge(pool_step, n[0])
            g.affine_select(out=ident[:], in_=ident[:], compare_op=ALU.not_equal, fill=1.0, base=0,
                            pattern=[[-1, P]], channel_multiplier=1).then_inc(ident_ready, 1)
            link(g.affine_select(out=tri_incl[:], in_=ones[:], compare_op=ALU.is_ge, fill=0.0, base=0,
                                 pattern=[[1, P]], channel_multiplier=-1))
            link(g.affine_select(out=tri_strict[:], in_=ones[:], compare_op=ALU.is_gt, fill=0.0, base=0,
                                 pattern=[[1, P]], channel_multiplier=-1))
            link(g.memset(far[:], 0.0))
            link(g.affine_select(out=far[:], in_=far[:], compare_op=ALU.is_ge, fill=BIG, base=0,
                                 pattern=[[1, P]], channel_multiplier=-1))
            link(g.iota(slot_iota[:], pattern=[[1, P]], base=0, channel_multiplier=0,
                        allow_small_or_imprecise_dtypes=True))
            link(g.memset(earlier[:], 1.0))
            link(g.affine_select(out=earlier[:], in_=earlier[:], compare_op=ALU.is_gt, fill=0.0, base=0,
                                 pattern=[[1, E], [-1, E]], channel_multiplier=0))
            link(g.memset(own_block[:], 1.0))
            link(g.affine_select(out=own_block[:], in_=own_block[:], compare_op=ALU.is_ge, fill=0.0, base=0,
                                 pattern=[[-QB, 32]], channel_multiplier=1))
            link(g.affine_select(out=own_block[:], in_=own_block[:], compare_op=ALU.is_ge, fill=0.0, base=QB - 1,
                                 pattern=[[QB, 32]], channel_multiplier=-1))
            pool.wait_ge(spatial_in, 32)
            g.memset(w_s[0:64, :, 64:P], 0.0).then_inc(consts_ready, 1)
            pool.wait_ge(ln_in, 32)
            for t in range(NT):
                pool.wait_ge(v_normed, t + 1)
                link(g.tensor_tensor(v[:, t, :], v[:, t, :], ln_g[:], ALU.mult))
                g.tensor_tensor(v[:, t, :], v[:, t, :], ln_b[:], ALU.add).then_inc(v_ready, 1)
            pool.wait_ge(mlstm_in, 16 * 5)
            pool.wait_ge(turned, 4 * (XR_MLSTM + 1))
            for i in range(KI // 4):
                if i:
                    pool.wait_ge(bd_used, i)
                for j in range(3):
                    o = blockdiag[:, j, :, :].rearrange("p c (m d) -> p c m d", d=QB)
                    for cc in range(4):
                        ins = g.tensor_tensor(
                            o[:, cc], qkv_w[:, j, 4 * i + cc, :].unsqueeze(1).to_broadcast([P, 32, QB]),
                            own_block[:].unsqueeze(2).to_broadcast([P, 32, QB]), ALU.mult)
                ins.then_inc(bd_ready, 1)
            pool.wait_ge(bd_used, 4)
            for c in range(KI):
                g.tensor_scalar(xc(c)[:, 0, :], xc(c)[:, 0, :], vec_a[:, (CONV + 2) * KI + c:(CONV + 2) * KI + c + 1], None,
                                ALU.mult).then_inc(skip_ready, 1)
            for t in range(NT):
                pool.wait_ge(hh_ready, t + 1)
                g.tensor_tensor(hl[:, t, :], xn[:, t, :], hh[:, t, :].bitcast(F32), ALU.subtract).then_inc(hl_ready, 1)

        @block.scalar
        def _(act):
            a = nc.scalar
            steps = [0]

            def link(ins):
                steps[0] += 1
                ins.then_inc(act_step, 1)
                act.wait_ge(act_step, steps[0])

            hi_next = [0]

            def split_hi(end):
                while hi_next[0] < end:
                    u = hi_next[0]
                    act.wait_ge(landed[slot_of(u)], 32 * (uses_before(u) + 1))
                    if u >= HIS:
                        act.wait_ge(unit_used, u - HIS + 1)
                    for half in HALVES:
                        a.copy(whi[:, u % HIS, half], raw[:, slot_of(u), half]).then_inc(hi_ready, 1)
                    hi_next[0] += 1

            def normalise(r):
                if r:
                    act.wait_ge(x_ready, NT * r - 1)
                else:
                    act.wait_ge(x_in, 16)
                a.activation(xn[:, 0, :], x[:, 0, :], ACT.Square, accum_out=ss[:, 0:1]).then_inc(squares, 1)

            def turn_hi(r, g0):
                for kp in range(KD // 2):
                    act.wait_ge(turned, (KD // 2) * r + kp + 1)
                    for k in (0, 1):
                        ins = a.activation(hTh[:, 2 * kp + k, :], ps[4 + kp][:, T * k:T * (k + 1)], ACT.Copy,
                                           scale=vec_b[:, g0 + 2 * kp + k:g0 + 2 * kp + k + 1])
                    ins.then_inc(hi_turned, 1)

            def rows(dst, r0, src, arrived):
                n = src.shape[0] * src.shape[1] // P
                act.dma_start(dst[r0:r0 + n, :], src.rearrange("j (k p) -> (j k) p", p=P)).then_inc(arrived, 16)

            for j, name in enumerate(("norm_mix", "norm_ffn", "norm_ple")):
                rows(rows_b, 2 * KD * j, A[name], gain_rows_in)
            normalise(XR_GMLP)
            split_hi(1)
            act.wait_ge(prep_turned, 1)
            a.copy(vec_b[:], ps[1][:, 0:6 * KD]).then_inc(gains_copied, 1)
            act.wait_ge(gains_copied, 1)
            turn_hi(XR_GMLP, 0)
            rows(rows_a, 0, A["mb_conv_w"][0], rows_in)
            for j, name in enumerate(("mb_conv_b", "mb_norm_g", "mb_skip")):
                rows(rows_a, KI * (CONV + j), A[name], rows_in)
            act.dma_start(w_s[:], A["ga_w_s"][0].rearrange("g t s -> t g s")).then_inc(spatial_in, 16)
            act.dma_start(b_s[:], A["ga_b_s"][0].rearrange("g t -> (g t)").partition_broadcast(P)
                          .rearrange("p (g t) -> p g t", g=G)).then_inc(spatial_in, 16)
            def gate_hi(g):
                act.wait_ge(gated, g + 1)
                a.copy(ghi[:, :, 2 * g:2 * g + 2, :],
                       gprod[:, g % 2].rearrange("p c n t -> p n c t")).then_inc(gated_hi, 1)

            split_hi(U_GIN + 3)
            act.dma_start(ln_g[:], A["ga_ln_g"][0].partition_broadcast(P)).then_inc(ln_in, 16)
            act.dma_start(ln_b[:], A["ga_ln_b"][0].partition_broadcast(P)).then_inc(ln_in, 16)
            for j, name in enumerate(("mb_wq", "mb_wk", "mb_wv")):
                act.dma_start(qkv_w[:, j, :, :], A[name][0].rearrange("(c n) i d -> (n i) c d", n=32)).then_inc(mlstm_in, 16)
            act.dma_start(w_gate[:], A["mb_w_gate"][0].rearrange("(k p) n -> p k n", p=P)).then_inc(mlstm_in, 16)
            act.dma_start(b_gate[:], A["mb_b_gate"]).then_inc(mlstm_in, 16)
            act.dma_start(router[:], A["fe_router"][0].rearrange("(k p) e -> p k e", p=P)).then_inc(gain_in, 16)
            for i in range(4):
                act.wait_ge(unit_used, U_GIN + 2 * i + 2)
                split_hi(U_GIN + 2 * i + 4)
                for t in range(NT):
                    a.activation(v[:, t, i * CW:(i + 1) * CW], ps[2 * (i % 2) + t][:], ACT.Gelu).then_inc(v_gelu, 1)
                split_hi(U_GIN + 2 * i + 5)
            for i in range(4):
                un = U_GIN + 8 + 2 * i + 2
                act.wait_ge(unit_used, un)
                split_hi(un + 2)
                for b in range(2):
                    a.activation(uT[:, 4 * i + 2 * b:4 * i + 2 * b + 2, :], ps[2 * (i % 2) + b][:], ACT.Gelu).then_inc(u_gelu, 1)
                split_hi(un + 3)
                if i >= 2:
                    gate_hi(2 * i - 4)
                    gate_hi(2 * i - 3)
            for g in range(G):
                if g >= 4:
                    gate_hi(g)
                split_hi(min(U_GOUT + g + 3, U_FFN))
            split_hi(U_FFN + 1)

            normalise(XR_FFN)
            turn_hi(XR_FFN, 2 * KD)
            split_hi(U_FFN + 3)

            def embedding_hi(l):
                act.wait_ge(p_turned, l + 1)
                a.copy(pTh[:].rearrange("p k t -> p (k t)"), ps[3][:]).then_inc(p_hi, 1)

            def ffn_hi(base_unit):
                act.dma_start(p_tok[:], A["p"][0, 0].rearrange("(t p) n -> p t n", p=P)).then_inc(p_in[0], 16)
                for b in range(NB + 2):
                    if b < NB:
                        un = base_unit + gu_pos[b] + 2
                        split_hi(un + 1)
                        act.wait_ge(unit_used, un)
                        if b == 0:
                            act.wait_ge(rstd_ready, RSTD_NTH[XR_FFN] + 1)
                        for t in range(NT):
                            a.activation(sg[:, t, :], ps[t][:, 0:FB], ACT.Silu, scale=rstd[:, t:t + 1]).then_inc(silu_done, 1)
                        split_hi(un + 2)
                    if 1 <= b <= NB:
                        act.wait_ge(hid_turned, b)
                        a.copy(hidTh[:, (b - 1) % 2].rearrange("p j t -> p (j t)"), ps[2][:]).then_inc(hidT_hi, 1)
                    if b >= 2:
                        split_hi(base_unit + down_pos[b - 2] + 2)
                    if b == NB - 2:
                        embedding_hi(0)

            ffn_hi(U_FFN)

            def ple(l, r, base_unit, g0, end):
                normalise(r)
                turn_hi(r, g0)
                split_hi(end)
                act.wait_ge(rstd_ready, RSTD_NTH[r] + 1)
                for t in range(NT):
                    for h in range(2):
                        if 2 * t + h < 3:
                            act.wait_ge(sums, 3 * (2 + 2 * l) + 2 * t + h + 1)
                        else:
                            act.wait_ge(unit_used, base_unit + 5)
                        a.activation(psig[:, t, h * CW:(h + 1) * CW], ps[4 + 2 * t + h][:], ACT.Sigmoid,
                                     scale=rstd[:, t:t + 1]).then_inc(ple_sig, 1)

            ple(0, XR_PLE0, U_PLE0, 4 * KD, U_MIN + 1)

            def mlstm():
                normalise(XR_MLSTM)
                split_hi(U_MIN + 3)
                turn_hi(XR_MLSTM, KD)

                def copy_qk(i):
                    for pr in range(2):
                        for j, dst in enumerate((qT, kT)):
                            item = (2 * i + pr) * 4 + j
                            act.wait_ge(qkv_mm, item + 1)
                            c = 4 * i + 2 * pr
                            a.copy(dst[:, c:c + 2, :].rearrange("p c t -> p (c t)"), ps[4 + item % 3][:]).then_inc(qk_copied, 1)

                for i in range(4):
                    un = U_MIN + 2 * i + 2
                    act.wait_ge(unit_used, un)
                    split_hi(un + 2)
                    if i:
                        copy_qk(i - 1)
                        act.wait_ge(bd_used, i)
                    split_hi(un + 3)
                    if not i:
                        act.wait_ge(pad_ready, 1)
                    for b in range(2):
                        ins = a.copy(xpad[:, 2 * b:2 * b + 2, CONV - 1:], ps[2 * (i % 2) + b][:].rearrange("p (c t) -> p c t", c=2))
                    ins.then_inc(xm_copied, 1)
                    act.wait_ge(xm_copied, i + 1)
                    for cc in range(4):
                        c = 4 * i + cc
                        ins = a.activation(xc(c)[:, 0, :], xpad[:, cc, 0:T], ACT.Identity, scale=vec_a[:, c:c + 1],
                                           bias=vec_a[:, CONV * KI + c:CONV * KI + c + 1])
                    ins.then_inc(conv_first, 1)
                    act.wait_ge(conv_done, i + 1)
                    a.activation(xc(4 * i, 4), xc(4 * i, 4), ACT.Silu).then_inc(xc_ready, 1)

                def take_z(i):
                    act.wait_ge(unit_used, U_MIN + 8 + 2 * i + 2)
                    for b in range(2):
                        a.copy(sz(4 * i + 2 * b, 2), ps[Z_BANKS[i] + b][:].rearrange("p (c t) -> p c t", c=2)).then_inc(z_copied, 1)

                take_z(0)
                split_hi(U_MIN + 12)
                copy_qk(3)
                act.wait_ge(forget_in, 1)
                link(a.activation(gate_e[:], gate_t[:], ACT.Exp))
                a.activation(gate_t[:], gate_e[:], ACT.Ln, bias=1.0).then_inc(forget_ln, 1)
                split_hi(U_MIN + 13)
                take_z(1)
                split_hi(U_MIN + 15)
                act.wait_ge(m_tok_ready, 1)
                a.activation(emt[:], emt[:], ACT.Exp, scale=-1.0).then_inc(emt_ready, 1)

                def decay(h):
                    act.wait_ge(arg_ready, h + 1)
                    if h >= 2:
                        act.wait_ge(p_weights, h - 1)
                    a.activation(wexp[:, h % 2, :], arg[:], ACT.Exp, scale=-1.0).then_inc(decay_ready, 1)

                def take_num(h):
                    act.wait_ge(num_mm, h + 1)
                    a.copy(num[:, h].rearrange("p t d -> p (t d)"), ps[2][:]).then_inc(num_copied, 1)
                    a.copy(qn[:, :, h], ps[3][:, 0:NT]).then_inc(qn_copied, 1)

                for h in range(H):
                    decay(h)
                    if h:
                        take_num(h - 1)
                    if h == 3:
                        take_z(2)
                    if h in (1, 3, 5):
                        split_hi(U_MIN + 16 + h // 2)
                take_num(H - 1)

                def gate_z(g):
                    a.activation(sz(2 * g, 2), sz(2 * g, 2), ACT.Sigmoid).then_inc(z_ready, 1)

                def take_mixed(g):
                    act.wait_ge(mixed_ready, g + 1)
                    a.copy(ohi[:, 2 * g:2 * g + 2, :], otmp[:, g % 2]).then_inc(mixed_hi, 1)

                act.wait_ge(z_copied, 6)
                gate_z(0)
                gate_z(1)
                take_mixed(0)
                gate_z(2)
                take_mixed(1)
                take_z(3)
                split_hi(U_MOUT + 3)
                take_mixed(2)
                act.wait_ge(z_copied, 8)
                for g in range(3, H):
                    gate_z(g)
                for g in range(3, H):
                    split_hi(U_MOUT + g + 1)
                    take_mixed(g)
                split_hi(U_MOE + 1)

            mlstm()

            def experts():
                act.dma_start(g_row[:], A["norm_ffn"][1].partition_broadcast(P)).then_inc(gain_in, 16)
                normalise(XR_MOE)
                split_hi(U_MOE + 2)
                for kp in (0, 2):
                    act.wait_ge(turned, (KD // 2) * XR_MOE + kp + 1)
                    for k in (2 * kp, 2 * kp + 1):
                        ins = a.activation(hT32[:, k, :], ps[4 + kp][:, (k % 2) * T:(k % 2 + 1) * T], ACT.Copy,
                                           scale=vec_b[:, 3 * KD + k:3 * KD + k + 1])
                    ins.then_inc(hT32_even, 1)
                for t in range(NT):
                    act.wait_ge(h_gained, t + 1)
                    a.copy(hh[:, t, :], xn[:, t, :]).then_inc(hh_ready, 1)
                act.wait_ge(chosen_ready, 2)
                a.activation(prob[:, 0, :], top[:, 0, :], ACT.Exp).then_inc(prob_exp, 1)
                split_hi(U_MOE + 3)
                act.dma_start(p_tok[:], A["p"][1, 0].rearrange("(t p) n -> p t n", p=P)).then_inc(p_in[1], 16)

                act.wait_ge(over_known, 1)
                with act.If(act.value_load(over[0:1, 0:1], min_val=0, max_val=1) > 0):
                    with act.Fori(0, E) as e:
                        with act.Fori(0, NB) as b:
                            act.wait_ge(o_y_added, e * NB + b + 1)
                            for w, dst in (("fe_w_gate", o_gate), ("fe_w_up", o_up)):
                                act.dma_start(dst[:], A[w][0, e].rearrange("(k p) f -> p k f", p=P)[:, :, bass.ds(b * FB, FB)]
                                              ).then_inc(o_landed, 16)
                            act.dma_start(o_down[:], A["fe_w_down"][0, e].rearrange("(f k p) n -> f p k n", k=2, p=P)[b]
                                          ).then_inc(o_landed, 16)
                            act.wait_ge(o_gu_mm, e * NB + b + 1)
                            a.activation(o_sg[:], ps[0][:, 0:FB], ACT.Silu).then_inc(o_silu, 1)
                    act.wait_ge(o_added, 4 * E)

                def gathered_hi(e, o):
                    for b in range(2):
                        act.wait_ge(e_gathered, e * 2 + (2 * o + b + 1))
                        a.copy(xgh[:, 4 * b:4 * b + 4, :].rearrange("p k s -> p (k s)"), ps[6 + b][:]).then_inc(e_xg_hi, 1)

                def y_hi(e):
                    act.wait_ge(unit_used, e * FU + (U_MOE + FU))
                    for b in range(2):
                        a.activation(yh[:, b * CW:(b + 1) * CW], ps[4 + b][:], ACT.Copy, scale=c_slot[:, 0:1]).then_inc(e_y_hi, 1)

                def blocks(e, o, span, more):
                    def split_e(end):
                        while hi_next[0] < end + o * FU:
                            j = hi_next[0]
                            s = j % SLOTS
                            act.wait_ge(landed[s], e * (32 * FU // SLOTS) + 32 * (early_uses[s] + j // SLOTS + 1))
                            act.wait_ge(unit_used, e * FU + (U_MOE + j - HIS + 1))
                            for half in HALVES:
                                a.copy(whi[:, (U_MOE + j) % HIS, half], raw[:, s, half]).then_inc(hi_ready, 1)
                            hi_next[0] += 1

                    for b in span:
                        if b < NB:
                            un = gu_pos[b] + 2
                            split_e(un + 2)
                            act.wait_ge(unit_used, e * FU + (U_MOE + o * FU + un))
                            a.activation(sg[:, b % 2, :], ps[b % 2][:, 0:FB], ACT.Silu).then_inc(e_silu, 1)
                            if b == NB - 1:
                                split_e(un + 3)
                        if 1 <= b <= NB:
                            act.wait_ge(e_hid_turned, e * NB + (o * NB + b))
                            a.copy(hidTh[:, (b - 1) % 2, :, 0:P], ps[2][:, 0:2 * P].rearrange("p (j t) -> p j t", j=2)).then_inc(e_hidT_hi, 1)
                        if b == NB and more:
                            gathered_hi(e, o + 1)
                        if b == GATHER_AT and not more:
                            embedding_hi(1)
                        if b == SPLIT_AT - 1:
                            act.wait_ge(e_pickT_mm, e + (o + 1))
                            a.copy(pickT[:].rearrange("p t s -> p (t s)"), ps[3][:, 0:T]).then_inc(e_pickT, 1)
                        if b >= NB:
                            split_e(down_pos[b - 2] + 3)

                gathered_hi(0, 0)
                hi_next[0] = HIS
                blocks(0, 0, range(SPLIT_AT), True)
                start = hi_next[0]
                with act.Fori(0, E - 1) as e:
                    hi_next[0] = start
                    blocks(e, 0, range(SPLIT_AT, NB + 2), True)
                    y_hi(e)
                    blocks(e, 1, range(SPLIT_AT), True)
                assert hi_next[0] == start + FU
                hi_next[0] = start
                blocks(E - 1, 0, range(SPLIT_AT, NB + 2), False)
                y_hi(E - 1)
                hi_next[0] += U_MOE + (E - 1) * FU

            experts()
            ple(1, XR_PLE1, U_PLE1, 5 * KD, U_PLE1 + 5)
            act.dma_start(g_row[:], A["norm_final"].partition_broadcast(P)).then_inc(final_in, 16)
            normalise(XR_FINAL)
            for t in range(NT):
                act.wait_ge(xn_ready, NT * XN_NTH[XR_FINAL] + t + 1)
                act.dma_start(out[0, t * P:(t + 1) * P, :], xn[:, t, :]).then_inc(out_done, 16)

        @block.vector
        def _(dve):
            d = nc.vector
            steps = [0]

            def link(ins):
                steps[0] += 1
                ins.then_inc(dve_step, 1)
                dve.wait_ge(dve_step, steps[0])

            lo_next = [0]

            def split_lo(end):
                while lo_next[0] < end:
                    u = lo_next[0]
                    for n, half in enumerate(HALVES):
                        dve.wait_ge(hi_ready, 2 * u + n + 1)
                        d.tensor_tensor(wlo[:, slot_of(u), half], raw[:, slot_of(u), half], whi[:, u % HIS, half].bitcast(F32),
                                        ALU.subtract).then_inc(lo_ready, 1)
                    lo_next[0] += 1

            def rsqrt(y, v_in, tmp, done=None):
                link(d.tensor_scalar(y.bitcast(I32), v_in.bitcast(I32), -0.5, RSQRT_SEED, ALU.mult, ALU.add))
                for step in range(3):
                    link(d.scalar_tensor_tensor(out=tmp, in0=y, scalar=-0.5, in1=y, op0=ALU.mult, op1=ALU.mult))
                    link(d.tensor_tensor(tmp, tmp, v_in, ALU.mult))
                    ins = d.scalar_tensor_tensor(out=y, in0=tmp, scalar=1.5, in1=y, op0=ALU.add, op1=ALU.mult)
                    if step == 2 and done is not None:
                        ins.then_inc(done, 1)
                    else:
                        link(ins)

            def normalise(r):
                if r:
                    dve.wait_ge(x_ready, NT * r)
                else:
                    dve.wait_ge(x_in2, 16)
                link(d.tensor_tensor_reduce(xn[:, 1, :], x[:, 1, :], x[:, 1, :], 1.0, 0.0, ALU.mult, ALU.add, ss[:, 1:2]))
                if r == XR_MOE:
                    turn_router_side()
                dve.wait_ge(squares, r + 1)
                link(d.tensor_scalar(var[:], ss[:], 1.0 / D, EPS, ALU.mult, ALU.add))
                rsqrt(rstd[:], var[:], newton[:, 0:NT], rstd_ready if r in RSTD_NTH else None)
                if r in RSTD_NTH:
                    dve.wait_ge(rstd_ready, RSTD_NTH[r] + 1)
                for t in range(NT):
                    if r == XR_FINAL:
                        if not t:
                            dve.wait_ge(final_in, 16)
                        d.scalar_tensor_tensor(out=xn[:, t, :], in0=x[:, t, :], scalar=rstd[:, t:t + 1], in1=g_row[:],
                                               op0=ALU.mult, op1=ALU.mult).then_inc(xn_ready, 1)
                    elif r == XR_MOE:
                        if not t:
                            dve.wait_ge(gain_in, 32)
                        d.scalar_tensor_tensor(out=xn[:, t, :], in0=x[:, t, :], scalar=rstd[:, t:t + 1], in1=g_row[:],
                                               op0=ALU.mult, op1=ALU.mult).then_inc(h_gained, 1)
                    elif r in XN_NTH:
                        d.tensor_scalar(xn[:, t, :], x[:, t, :], rstd[:, t:t + 1], None, ALU.mult).then_inc(xn_ready, 1)

            def turn_router_side():
                for kp in (1, 3):
                    dve.wait_ge(turned, (KD // 2) * XR_MOE + kp + 1)
                    for k in (2 * kp, 2 * kp + 1):
                        ins = d.tensor_scalar(hT32[:, k, :], ps[4 + kp][:, (k % 2) * T:(k % 2 + 1) * T],
                                              vec_b[:, 3 * KD + k:3 * KD + k + 1], None, ALU.mult)
                    ins.then_inc(hT32_odd, 1)

            def turn_lo(r, g0, nth):
                for kp in range(KD // 2):
                    dve.wait_ge(hi_turned, (KD // 2) * nth + kp + 1)
                    for k in (0, 1):
                        kk = 2 * kp + k
                        ins = d.scalar_tensor_tensor(out=hTl[:, kk, :], in0=ps[4 + kp][:, T * k:T * (k + 1)],
                                                     scalar=vec_b[:, g0 + kk:g0 + kk + 1], in1=hTh[:, kk, :].bitcast(F32),
                                                     op0=ALU.mult, op1=ALU.subtract)
                    ins.then_inc(h_ready, 1)

            def embedding_lo(l):
                dve.wait_ge(p_hi, l + 1)
                d.tensor_tensor(pTl[:].rearrange("p k t -> p (k t)"), ps[3][:],
                                pTh[:].rearrange("p k t -> p (k t)").bitcast(F32), ALU.subtract).then_inc(p_ready, 1)

            def add_to_x(b0, nth, end):
                for t in range(NT):
                    for h in range(2):
                        if 2 * t + h < 3:
                            dve.wait_ge(sums, 3 * nth + 2 * t + h + 1)
                        else:
                            dve.wait_ge(unit_used, end)
                        xs = x[:, t, h * CW:(h + 1) * CW]
                        ins = d.tensor_tensor(xs, xs, ps[b0 + 2 * t + h][:], ALU.add)
                    ins.then_inc(x_ready, 1)

            normalise(XR_GMLP)
            split_lo(1)
            dve.wait_ge(gains_copied, 1)
            turn_lo(XR_GMLP, 0, 0)
            split_lo(U_GIN + 3)
            for i in range(4):
                split_lo(U_GIN + 2 * i + 4)
                for t in range(NT):
                    dve.wait_ge(v_gelu, NT * i + t + 1)
                    ins = d.bn_stats(ln_stats[:, t, i, :], v[:, t, i * CW:(i + 1) * CW])
                link(ins)
                split_lo(U_GIN + 2 * i + 5)
                if i == 2:
                    dve.wait_ge(prep_turned, 4)
                    d.tensor_copy(vec_a[:], ps[4][:, 0:(CONV + 3) * KI]).then_inc(prep_copied, 1)
                    d.tensor_copy(w_sT[:, 0:4, :].rearrange("p g t -> p (g t)"), ps[5][:]).then_inc(prep_copied, 1)
                    d.tensor_copy(w_sT[:, 4:8, :].rearrange("p g t -> p (g t)"), ps[6][:]).then_inc(prep_copied, 1)
            for t in range(NT):
                link(d.bn_aggr(ln_mv[:, t, :], ln_stats[:, t].rearrange("p i s -> p (i s)")))
            link(d.tensor_scalar(var[:], ln_mv[:, :, 1], EPS, None, ALU.add))
            rsqrt(rstd[:], var[:], newton[:, 0:NT])
            for t in range(NT):
                d.tensor_scalar(v[:, t, :], v[:, t, :], ln_mv[:, t, 0:1], rstd[:, t:t + 1],
                                ALU.subtract, ALU.mult).then_inc(v_normed, 1)
            def gate(g):
                dve.wait_ge(mixed, g + 1)
                link(d.tensor_tensor(gtmp[:].rearrange("p c n t -> p (c n) t"), ps[4 + g % 4][:].rearrange("p (c t) -> p c t", c=4),
                                     b_s[:, g, :].unsqueeze(1).to_broadcast([P, 4, P]), ALU.add))
                dve.wait_ge(u_gelu, g + 1)
                d.tensor_tensor(gprod[:, g % 2].rearrange("p c n t -> p (c n t)"), gtmp[:].rearrange("p c n t -> p (c n t)"),
                                uT[:, 2 * g:2 * g + 2, :].rearrange("p c t -> p (c t)"), ALU.mult).then_inc(gated, 1)
                dve.wait_ge(gated_hi, g + 1)
                d.tensor_tensor(glo[:, 2 * g:2 * g + 2, :].rearrange("p c (n t) -> p c n t", n=NT).rearrange("p c n t -> p n c t"),
                                gprod[:, g % 2].rearrange("p c n t -> p n c t"),
                                ghi[:, :, 2 * g:2 * g + 2, :].bitcast(F32), ALU.subtract).then_inc(gated_lo, 1)

            for i in range(4):
                split_lo(U_GIN + 8 + 2 * i + 5)
                if i >= 2:
                    gate(2 * i - 4)
                    gate(2 * i - 3)
            for g in range(G):
                if g >= 4:
                    gate(g)
                split_lo(min(U_GOUT + g + 3, U_FFN))
            split_lo(U_FFN + 1)
            add_to_x(0, 0, U_FFN)

            turn_lo(XR_FFN, 2 * KD, 1)
            split_lo(U_FFN + 2)
            normalise(XR_FFN)
            split_lo(U_FFN + 3)
            for b in range(NB + 2):
                if b < NB:
                    un = U_FFN + gu_pos[b] + 2
                    split_lo(un + 1)
                    for t in range(NT):
                        dve.wait_ge(silu_done, NT * b + t + 1)
                        d.scalar_tensor_tensor(out=hid[:, b % 2, t, :], in0=ps[t][:, FB:2 * FB], scalar=rstd[:, t:t + 1],
                                               in1=sg[:, t, :], op0=ALU.mult, op1=ALU.mult).then_inc(hid_ready, 1)
                    split_lo(un + 2)
                if 1 <= b <= NB:
                    dve.wait_ge(hidT_hi, b)
                    d.tensor_tensor(hidTl[:, (b - 1) % 2].rearrange("p j t -> p (j t)"), ps[2][:],
                                    hidTh[:, (b - 1) % 2].rearrange("p j t -> p (j t)").bitcast(F32), ALU.subtract).then_inc(hidT_lo, 1)
                if b >= 2:
                    split_lo(U_FFN + down_pos[b - 2] + 2)
                if b == NB - 2:
                    embedding_lo(0)
            add_to_x(4, 1, U_PLE0)

            def ple(l, r, base_unit, g0, nth, end):
                turn_lo(r, g0, nth)
                split_lo(base_unit + 2)
                normalise(r)
                split_lo(end)
                for t in range(NT):
                    for h in range(2):
                        dve.wait_ge(ple_sig, 4 * l + 2 * t + h + 1)
                        s = psig[:, t, h * CW:(h + 1) * CW]
                        link(d.tensor_tensor(s, s, ps[2 * t + h][:], ALU.mult))
                        xs = x[:, t, h * CW:(h + 1) * CW]
                        ins = d.tensor_tensor(xs, xs, s, ALU.add)
                    ins.then_inc(x_ready, 1)

            ple(0, XR_PLE0, U_PLE0, 4 * KD, 2, U_MIN + 1)

            newton3 = newton[:].rearrange("p (t h) -> p t h", t=NT)

            def mlstm():
                normalise(XR_MLSTM)
                split_lo(U_MIN + 2)
                turn_lo(XR_MLSTM, KD, 3)
                d.memset(xpad[:, :, 0:CONV - 1], 0.0).then_inc(pad_ready, 1)
                split_lo(U_MIN + 3)

                def copy_v(i):
                    for pr in range(2):
                        c = 4 * i + 2 * pr
                        item = (2 * i + pr) * 4 + 2
                        dve.wait_ge(qkv_mm, item + 1)
                        d.tensor_copy(vT[:].rearrange("p c t -> p (c t)"), ps[4 + item % 3][:]).then_inc(v_copied, 1)
                        dve.wait_ge(qkv_mm, item + 2)
                        d.tensor_copy(v_m[:, :, c * P:(c + 2) * P], ps[4 + (item + 1) % 3][:].rearrange("p (t f) -> p t f", t=NT)).then_inc(v_copied, 1)

                for i in range(4):
                    un = U_MIN + 2 * i + 2
                    split_lo(un + 2)
                    if i:
                        copy_v(i - 1)
                    split_lo(un + 3)
                    dve.wait_ge(conv_first, i + 1)
                    for j in range(1, CONV):
                        for cc in range(4):
                            c = 4 * i + cc
                            ins = d.scalar_tensor_tensor(out=xc(c)[:, 0, :], in0=xpad[:, cc, j:j + T],
                                                         scalar=vec_a[:, KI * j + c:KI * j + c + 1], in1=xc(c)[:, 0, :],
                                                         op0=ALU.mult, op1=ALU.add)
                        if j < CONV - 1:
                            link(ins)
                    ins.then_inc(conv_done, 1)
                split_lo(U_MIN + 12)
                copy_v(3)
                dve.wait_ge(gates_mm, 1)
                link(d.tensor_copy(gates[:].rearrange("p t g -> p (t g)"), ps[7][:, 0:NT * 2 * H]))
                link(d.tensor_scalar(gate_t[:], gates[:, :, H:], -1.0, None, ALU.mult))
                d.tensor_tensor(gate_t[:], gate_t[:], gates[:, :, H:], ALU.min).then_inc(forget_in, 1)
                for i in range(2):
                    d.memset(scan[i][:, 0:P], 0.0).then_inc(dve_step, 1)
                steps[0] += 2
                split_lo(U_MIN + 13)
                dve.wait_ge(forget_ln, 1)
                d.scalar_tensor_tensor(out=logf[:], in0=gates[:, :, H:], scalar=0.0, in1=gate_t[:],
                                       op0=ALU.min, op1=ALU.subtract).then_inc(logf_ready, 1)
                dve.wait_ge(cums_mm, 1)
                link(d.tensor_copy(b_tok[:].rearrange("p t h -> p (t h)"), ps[7][:, 64:64 + NT * H]))
                d.tensor_tensor(a_tok[:], gates[:, :, 0:H], b_tok[:], ALU.subtract).then_inc(a_ready, 1)
                dve.wait_ge(a_turned, 1)
                link(d.tensor_copy(scan[0][:, P:], ps[7][0:H, 256:256 + T]))
                cur = 0
                s = 1
                while s < T:
                    ins = d.tensor_tensor(scan[1 - cur][:, P:], scan[cur][:, P:], scan[cur][:, P - s:P - s + T], ALU.max)
                    cur = 1 - cur
                    s *= 2
                    if s < T:
                        link(ins)
                assert cur == 0
                ins.then_inc(m_ready, 1)
                split_lo(U_MIN + 14)
                dve.wait_ge(m_turned, 1)
                d.tensor_tensor(emt[:], b_tok[:], ps[7][:, 96:96 + NT * H].rearrange("p (t h) -> p t h", t=NT), ALU.add).then_inc(m_tok_ready, 1)

                def decay(h):
                    dve.wait_ge(scores_mm, h + 1)
                    if h:
                        dve.wait_ge(decay_ready, h)
                    mb = ps[6 + h % 2]
                    d.scalar_tensor_tensor(out=arg[:, 0:P], in0=mb[:, 0:P], scalar=a_tok[:, 0, h:h + 1], in1=far[:],
                                           op0=ALU.subtract, op1=ALU.max)
                    d.tensor_scalar(arg[:, P:2 * P], mb[:, P:2 * P], a_tok[:, 0, h:h + 1], 0.0, ALU.subtract, ALU.max)
                    d.scalar_tensor_tensor(out=arg[:, 2 * P:], in0=mb[:, P:2 * P], scalar=a_tok[:, 1, h:h + 1], in1=far[:],
                                           op0=ALU.subtract, op1=ALU.max).then_inc(arg_ready, 1)
                    dve.wait_ge(decay_ready, h + 1)
                    if h >= 2:
                        dve.wait_ge(num_mm, h - 1)
                    d.scalar_tensor_tensor(out=pT[:, h % 2, :], in0=ps[4 + h % 2][:, 0:3 * P], scalar=DH ** -0.5,
                                           in1=wexp[:, h % 2, :], op0=ALU.mult, op1=ALU.mult).then_inc(p_weights, 1)

                def stats(h):
                    dve.wait_ge(num_copied, h + 1)
                    for t in range(NT):
                        ins = d.bn_stats(head_stats[:, t, h, :], num[:, h, t, :])
                    link(ins)
                    for t in range(NT):
                        ins = d.bn_aggr(head_mv[:, t, h, :], head_stats[:, t, h, :])
                    link(ins)

                def norm_heads(b):
                    hs = slice(4 * b, 4 * b + 4)
                    r, v2, sc, tmp = head_r[:, :, hs], head_v[:, :, hs], head_s[:, :, hs], newton3[:, :, hs]
                    dve.wait_ge(qn_copied, 4 * b + 4)
                    dve.wait_ge(emt_ready, 1)
                    link(d.scalar_tensor_tensor(out=r, in0=qn[:, :, hs], scalar=-1.0, in1=emt[:, :, hs], op0=ALU.mult, op1=ALU.max))
                    link(d.tensor_tensor(r, r, qn[:, :, hs], ALU.max))
                    link(d.reciprocal(r, r))
                    link(d.tensor_tensor(v2, r, r, ALU.mult))
                    link(d.tensor_tensor(v2, v2, head_mv[:, :, hs, 1], ALU.mult))
                    link(d.tensor_scalar(v2, v2, EPS, None, ALU.add))
                    rsqrt(sc, v2, tmp)
                    link(d.tensor_tensor(sc, sc, r, ALU.mult))
                    for h in range(4 * b, 4 * b + 4):
                        for t in range(NT):
                            ins = d.tensor_scalar(num[:, h, t, :], num[:, h, t, :], head_mv[:, t, h, 0:1], head_s[:, t, h:h + 1],
                                                  ALU.subtract, ALU.mult)
                        ins.then_inc(hn_ready, 1)

                def mix_out(g):
                    dve.wait_ge(hn_turned, g + 1)
                    dve.wait_ge(skip_ready, 2 * g + 2)
                    for k in range(2):
                        c = 2 * g + k
                        ins = d.scalar_tensor_tensor(out=otmp[:, g % 2, k, :], in0=ps[4 + g % 4][:, k * T:(k + 1) * T],
                                                     scalar=vec_a[:, (CONV + 1) * KI + c:(CONV + 1) * KI + c + 1], in1=xc(c)[:, 0, :],
                                                     op0=ALU.mult, op1=ALU.add)
                    link(ins)
                    dve.wait_ge(z_ready, g + 1)
                    d.tensor_tensor(otmp[:, g % 2], otmp[:, g % 2], sz(2 * g, 2), ALU.mult).then_inc(mixed_ready, 1)
                    dve.wait_ge(mixed_hi, g + 1)
                    d.tensor_tensor(olo[:, 2 * g:2 * g + 2, :], otmp[:, g % 2], ohi[:, 2 * g:2 * g + 2, :].bitcast(F32),
                                    ALU.subtract).then_inc(mixed_lo, 1)

                for h in range(H):
                    decay(h)
                    if h:
                        stats(h - 1)
                    if h == 1:
                        split_lo(U_MIN + 15)
                    if h in (2, 4):
                        split_lo(U_MIN + 15 + h // 2)
                    if h == 5:
                        norm_heads(0)
                split_lo(U_MOUT + 2)
                for g in range(3):
                    mix_out(g)
                split_lo(U_MOUT + 3)
                stats(H - 1)
                norm_heads(1)
                for g in range(3, H):
                    split_lo(U_MOUT + g + 1)
                    mix_out(g)
                add_to_x(0, 3, U_MOE)

            mlstm()

            def experts():
                normalise(XR_MOE)
                split_lo(U_MOE + 2)
                dve.wait_ge(logits_mm, 1)
                for t in range(NT):
                    ins = d.tensor_scalar(logits[:, t, :], ps[0][:, t * E:(t + 1) * E], rstd[:, t:t + 1], None, ALU.mult)
                link(ins)
                lj = logits[:].unsqueeze(2).to_broadcast([P, NT, E, E])
                le = logits[:].unsqueeze(3).to_broadcast([P, NT, E, E])
                d.tensor_tensor(cmp[:, 0], lj, le, ALU.is_gt).then_inc(dve_step, 1)
                steps[0] += 1
                link(d.tensor_tensor(cmp[:, 1], lj, le, ALU.is_equal))
                for t in range(NT):
                    ins = d.tensor_tensor(cmp[:, 1, t], cmp[:, 1, t], earlier[:], ALU.mult)
                link(ins)
                link(d.tensor_tensor(cmp[:, 0], cmp[:, 0], cmp[:, 1], ALU.add))
                link(d.tensor_reduce(rank[:], cmp[:, 0], AX.X, ALU.add))
                d.tensor_scalar(chosen[:], rank[:], 1.5, None, ALU.is_lt).then_inc(chosen_ready, 1)
                for j in range(2):
                    ins = d.tensor_scalar(sel[:, j], rank[:], float(j), None, ALU.is_equal)
                link(ins)
                for j in range(2):
                    ins = d.tensor_tensor(picked[:, j], sel[:, j], logits[:], ALU.mult)
                link(ins)
                link(d.tensor_reduce(top[:], picked[:], AX.X, ALU.add))
                d.tensor_tensor(top[:, 0, :], top[:, 1, :], top[:, 0, :], ALU.subtract).then_inc(chosen_ready, 1)
                dve.wait_ge(prob_exp, 1)
                link(d.tensor_scalar(prob[:, 1, :], prob[:, 0, :], 1.0, None, ALU.add))
                link(d.reciprocal(top[:, 0, :], prob[:, 1, :]))
                link(d.tensor_tensor(top[:, 1, :], top[:, 0, :], prob[:, 0, :], ALU.mult))
                for j in range(2):
                    for t in range(NT):
                        ins = d.tensor_scalar(sel[:, j, t, :], sel[:, j, t, :], top[:, j, t:t + 1], None, ALU.mult)
                link(ins)
                d.tensor_tensor(comb[:], sel[:, 0], sel[:, 1], ALU.add).then_inc(comb_ready, 1)
                dve.wait_ge(slots_mm, 1)
                link(d.tensor_scalar(slot[:], ps[1][:, 0:NT * E].rearrange("p (t e) -> p t e", t=NT), 1.0, None, ALU.add))
                link(d.tensor_tensor(slot[:], slot[:], chosen[:], ALU.mult))
                link(d.tensor_scalar(slot[:], slot[:], -1.0, None, ALU.add))
                link(d.tensor_reduce(most[:], ps[1][:, 2 * E:3 * E], AX.X, ALU.max))
                d.tensor_scalar(over[:], most[:], float(P), None, ALU.is_gt).then_inc(over_known, 1)
                dve.wait_ge(over_known, 1)
                with dve.If(dve.value_load(over[0:1, 0:1], min_val=0, max_val=1) > 0):
                    d.memset(o_y[:], 0.0).then_inc(o_y_added, 1)
                    dve.wait_ge(o_y_added, 1)
                    with dve.Fori(0, E) as e:
                        d.memset(o_y[:], 0.0).then_inc(o_picked, 1)
                        for t in range(NT):
                            d.tensor_scalar(o_pick[:, t, :], slot_iota[:], float(P), slot[:, t, bass.ds(e, 1)], ALU.add,
                                            ALU.is_equal).then_inc(o_picked, 1)
                        dve.wait_ge(o_gathered, e + 1)
                        d.tensor_copy(o_pickT[:].rearrange("p t s -> p (t s)"), ps[2][:, 0:T]).then_inc(o_copied, 1)
                        d.tensor_copy(c_slot[:], ps[2][:, T:T + 1]).then_inc(o_copied, 1)
                        for h in range(2):
                            d.tensor_copy(o_xg[:, 4 * h:4 * h + 4, :].rearrange("p k s -> p (k s)"), ps[6 + h][:]).then_inc(o_copied, 1)
                        with dve.Fori(0, NB) as b:
                            dve.wait_ge(o_silu, e * NB + b + 1)
                            d.tensor_tensor(o_hid[:], o_sg[:], ps[0][:, FB:2 * FB], ALU.mult).then_inc(o_hid_ready, 1)
                            dve.wait_ge(o_hid_turned, e * NB + b + 1)
                            d.tensor_copy(o_hidT[:].rearrange("p j s -> p (j s)"), ps[2][:, 0:T]).then_inc(o_hidT_ready, 1)
                            dve.wait_ge(o_down_mm, e * NB + b + 1)
                            dve.wait_ge(o_picked, e * 3 + 3)
                            d.tensor_tensor(o_y[:, 0:CW], o_y[:, 0:CW], ps[4][:], ALU.add).then_inc(o_y_ready, 1)
                            d.tensor_tensor(o_y[:, CW:], o_y[:, CW:], ps[5][:], ALU.add).then_inc(o_y_added, 1)
                            dve.wait_ge(o_y_added, e * NB + b + 2)
                            dve.wait_ge(o_y_ready, e * (NB + 1) + b + 1)
                        dve.wait_ge(o_copied, e * 4 + 4)
                        d.tensor_scalar(o_y[:], o_y[:], c_slot[:, 0:1], None, ALU.mult).then_inc(o_y_ready, 1)
                        for q in range(4):
                            dve.wait_ge(o_back, e * 4 + q + 1)
                            xs = x[:, q // 2, (q % 2) * CW:(q % 2 + 1) * CW]
                            d.tensor_tensor(xs, xs, ps[6 + q % 2][:], ALU.add).then_inc(o_added, 1)
                        dve.wait_ge(o_added, e * 4 + 4)
                    dve.wait_ge(o_added, 4 * E)

                def pick_tokens(e, o):
                    for t in range(NT):
                        d.tensor_scalar(pick[:, t, :], slot_iota[:], slot[:, t, bass.ds(e + o, 1)], None, ALU.is_equal).then_inc(e_pick, 1)

                def gathered_lo(e, o):
                    for b in range(2):
                        dve.wait_ge(e_xg_hi, e * 2 + (2 * o + b + 1))
                        d.tensor_tensor(xgl[:, 4 * b:4 * b + 4, :].rearrange("p k s -> p (k s)"), ps[6 + b][:],
                                        xgh[:, 4 * b:4 * b + 4, :].rearrange("p k s -> p (k s)").bitcast(F32),
                                        ALU.subtract).then_inc(e_xg_lo, 1)

                def y_lo(e):
                    for b in range(2):
                        dve.wait_ge(e_y_hi, e * 2 + (b + 1))
                        d.scalar_tensor_tensor(out=yl[:, b * CW:(b + 1) * CW], in0=ps[4 + b][:], scalar=c_slot[:, 0:1],
                                               in1=yh[:, b * CW:(b + 1) * CW].bitcast(F32), op0=ALU.mult, op1=ALU.subtract).then_inc(e_y_lo, 1)

                def add_back(e, t):
                    for h in range(2):
                        dve.wait_ge(e_back, e * 4 + (2 * t + h + 1))
                        xs = x[:, t, h * CW:(h + 1) * CW]
                        d.tensor_tensor(xs, xs, ps[6 + h][:], ALU.add).then_inc(e_added, 1)

                def blocks(e, o, span, more):
                    def split_e(end):
                        while lo_next[0] < end + o * FU:
                            j = lo_next[0]
                            s = j % SLOTS
                            for n, half in enumerate(HALVES):
                                dve.wait_ge(hi_ready, e * (2 * FU) + (2 * (U_MOE + j) + n + 1))
                                d.tensor_tensor(wlo[:, s, half], raw[:, s, half], whi[:, (U_MOE + j) % HIS, half].bitcast(F32),
                                                ALU.subtract).then_inc(lo_ready, 1)
                            lo_next[0] += 1

                    for b in span:
                        if b < NB:
                            split_e(gu_pos[b] + 4)
                            dve.wait_ge(e_silu, e * NB + (o * NB + b + 1))
                            d.tensor_tensor(hid[:, b % 2, 0, :], sg[:, b % 2, :], ps[b % 2][:, FB:2 * FB], ALU.mult).then_inc(e_hid, 1)
                            if b == NB - 1:
                                split_e(gu_pos[b] + 5)
                        if 1 <= b <= NB:
                            dve.wait_ge(e_hidT_hi, e * NB + (o * NB + b))
                            d.tensor_tensor(hidTl[:, (b - 1) % 2, :, 0:P], ps[2][:, 0:2 * P].rearrange("p (j t) -> p j t", j=2),
                                            hidTh[:, (b - 1) % 2, :, 0:P].bitcast(F32), ALU.subtract).then_inc(e_hidT_lo, 1)
                        if o and b in (1, 2):
                            add_back(e, b - 1)
                        if b == SPLIT_AT - 1:
                            dve.wait_ge(e_pickT, e + (o + 1))
                            d.tensor_copy(c_slot[:], ps[3][:, T:T + 1]).then_inc(e_pickT_c, 1)
                        if b == PICK_AT and more:
                            pick_tokens(e, o + 1)
                        if b == NB and more:
                            gathered_lo(e, o + 1)
                        if b == GATHER_AT and not more:
                            embedding_lo(1)
                        if b >= NB:
                            split_e(down_pos[b - 2] + 3)

                pick_tokens(0, 0)
                gathered_lo(0, 0)
                split_lo(U_MOE + HIS)
                lo_next[0] = HIS
                blocks(0, 0, range(SPLIT_AT), True)
                start = lo_next[0]
                with dve.Fori(0, E - 1) as e:
                    lo_next[0] = start
                    blocks(e, 0, range(SPLIT_AT, NB + 2), True)
                    y_lo(e)
                    blocks(e, 1, range(SPLIT_AT), True)
                assert lo_next[0] == start + FU
                lo_next[0] = start
                blocks(E - 1, 0, range(SPLIT_AT, NB + 2), False)
                y_lo(E - 1)
                for t in range(NT):
                    for h in range(2):
                        dve.wait_ge(e_back, 4 * (E - 1) + (2 * t + h + 1))
                        xs = x[:, t, h * CW:(h + 1) * CW]
                        ins = d.tensor_tensor(xs, xs, ps[(6, 4)[t] + h][:], ALU.add)
                    ins.then_inc(x_ready, 1)
                lo_next[0] += U_MOE + (E - 1) * FU

            experts()
            ple(1, XR_PLE1, U_PLE1, 5 * KD, 4, U_PLE1 + 5)
            normalise(XR_FINAL)

        @block.tensor
        def _(pe):
            m = nc.tensor

            def mm3(o, sh, sl, mh, ml, start, stop, **kw):
                m.matmul(o, sh, mh, start=start, stop=False, **kw)
                m.matmul(o, sl, mh, start=False, stop=False, **kw)
                return m.matmul(o, sh, ml, start=False, stop=stop, **kw)

            def hi(u):
                return whi[:, u % HIS, :]

            def lo(u):
                return wlo[:, slot_of(u), :]

            def turn(r):
                src = xn if r in XN_NTH else x
                for t in range(NT):
                    if r in XN_NTH:
                        pe.wait_ge(xn_ready, NT * XN_NTH[r] + t + 1)
                    elif r in (XR_FFN, XR_MOE):
                        pe.wait_ge(x_ready, NT * r - 1 + t)
                    else:
                        pe.wait_ge(x_ready, NT * r)
                    for k in range(KD):
                        ins = m.transpose(ps[4 + k // 2][:, (k % 2) * T + t * P:(k % 2) * T + (t + 1) * P], src[:, t, k * P:(k + 1) * P], ident[:])
                        if t == NT - 1 and k % 2 == 1:
                            ins.then_inc(turned, 1)

            def h_is(nth, k):
                pe.wait_ge(h_ready, (KD // 2) * nth + k // 2 + 1)

            def tokens_out(u0, banks, nth, first):
                for hf in range(2):
                    for t in range(NT):
                        for kk in range(4):
                            k = 4 * hf + kk
                            if t == 0 and kk % 2 == 0:
                                pe.wait_ge(lo_ready, 2 * (u0 + hf) + kk // 2 + 1)
                            if first and t == 0:
                                h_is(nth, k)
                            ins = mm3(ps[banks[t]][:], hTh[:, k, t * P:(t + 1) * P], hTl[:, k, t * P:(t + 1) * P],
                                      hi(u0 + hf)[:, kk * CW:(kk + 1) * CW], lo(u0 + hf)[:, kk * CW:(kk + 1) * CW],
                                      start=k == 0, stop=k == 7)
                    ins.then_inc(unit_used, 1)

            def features_out(u0, hf, banks, nth, first, cgs=range(4)):
                for cg in cgs:
                    for kk in range(4):
                        k = 4 * hf + kk
                        if cg == 0 and kk % 2 == 0:
                            pe.wait_ge(lo_ready, 2 * (u0 + hf) + kk // 2 + 1)
                        if first and cg == 0:
                            h_is(nth, k)
                        c0 = kk * CW + cg * P
                        ins = mm3(ps[banks[cg // 2]][:, (cg % 2) * T:(cg % 2 + 1) * T], hi(u0 + hf)[:, c0:c0 + P],
                                  lo(u0 + hf)[:, c0:c0 + P], hTh[:, k, :], hTl[:, k, :],
                                  start=k == 0 and cg % 2 == 0, stop=k == 7, skip_group_check=True)
                if 3 in cgs:
                    ins.then_inc(unit_used, 1)

            def rows_out(u, sh, sl, b0, first, last):
                def one(kk, t, h):
                    w0 = kk * D + h * CW
                    return mm3(ps[b0 + 2 * t + h][:], sh(kk, t), sl(kk, t), hi(u)[:, w0:w0 + CW], lo(u)[:, w0:w0 + CW],
                               start=first and kk == 0, stop=last and kk == 1)

                if last and not first:
                    pe.wait_ge(lo_ready, 2 * u + 2)
                    for t in range(NT):
                        for h in range(2):
                            for kk in range(2):
                                ins = one(kk, t, h)
                            if 2 * t + h < 3:
                                ins.then_inc(sums, 1)
                else:
                    for kk in range(2):
                        pe.wait_ge(lo_ready, 2 * u + kk + 1)
                        for t in range(NT):
                            for h in range(2):
                                ins = one(kk, t, h)
                ins.then_inc(unit_used, 1)

            pe.wait_ge(ident_ready, 1)
            pe.wait_ge(gain_rows_in, 16 * 3)
            m.transpose(ps[1][:, 0:6 * KD], rows_b[0:6 * KD, :], ident[0:6 * KD, 0:6 * KD]).then_inc(prep_turned, 1)

            turn(XR_GMLP)
            pe.wait_ge(gains_copied, 1)
            for i in range(4):
                if i >= 2:
                    pe.wait_ge(v_gelu, NT * (i - 1))
                tokens_out(U_GIN + 2 * i, (2 * (i % 2), 2 * (i % 2) + 1), 0, i == 0)
                if i == 1:
                    pe.wait_ge(rows_in, 16 * 4)
                    pe.wait_ge(consts_ready, 1)
                    na = (CONV + 3) * KI
                    m.transpose(ps[4][:, 0:na], rows_a[0:na, :], ident[0:na, 0:na]).then_inc(prep_turned, 1)
                    for b in range(2):
                        for g in range(4):
                            ins = m.transpose(ps[5 + b][:, g * P:(g + 1) * P], w_s[:, 4 * b + g, :], ident[:])
                        ins.then_inc(prep_turned, 1)
            def mix(g):
                if g >= 4:
                    pe.wait_ge(gated_lo, g - 3)
                pe.wait_ge(v_ready, NT)
                for c in range(2):
                    for n in range(NT):
                        cc = 2 * g + c
                        ins = m.matmul(ps[4 + g % 4][:, (c * NT + n) * P:(c * NT + n + 1) * P], v[:, n, cc * P:(cc + 1) * P],
                                       w_sT[:, g, :], start=True, stop=True)
                ins.then_inc(mixed, 1)

            for i in range(4):
                if i < 2:
                    pe.wait_ge(v_gelu, NT * (i + 3))
                else:
                    pe.wait_ge(u_gelu, 2 * (i - 1))
                if i == 3:
                    pe.wait_ge(prep_copied, 3)
                    for g in range(4):
                        mix(g)
                for hf in range(2):
                    features_out(U_GIN + 8 + 2 * i, hf, (2 * (i % 2), 2 * (i % 2) + 1), 0, False)

            pe.wait_ge(u_gelu, 8)
            for g in range(G):
                pe.wait_ge(gated_lo, g + 1)
                rows_out(U_GOUT + g, lambda kk, t: ghi[:, t, 2 * g + kk, :], lambda kk, t: glo[:, 2 * g + kk, t * P:(t + 1) * P],
                         0, g == 0, g == G - 1)
                if g + 4 < G:
                    mix(g + 4)

            def turn_embedding(l):
                pe.wait_ge(p_in[l], 16)
                for k in range(KP):
                    for t in range(NT):
                        ins = m.transpose(ps[3][:, k * T + t * P:k * T + (t + 1) * P], p_tok[:, t, k * P:(k + 1) * P], ident[:])
                ins.then_inc(p_turned, 1)

            def dense_ffn():
                turn(XR_FFN)
                for b in range(NB + 2):
                    if b < NB:
                        if b:
                            pe.wait_ge(hid_ready, NT * b)
                        for hf in range(2):
                            u = U_FFN + gu_pos[b] + hf
                            for t in range(NT):
                                for kk in range(4):
                                    k = 4 * hf + kk
                                    if t == 0 and kk % 2 == 0:
                                        pe.wait_ge(lo_ready, 2 * u + kk // 2 + 1)
                                    if b == 0 and t == 0:
                                        h_is(1, k)
                                    ins = mm3(ps[t][:], hTh[:, k, t * P:(t + 1) * P], hTl[:, k, t * P:(t + 1) * P],
                                              hi(u)[:, kk * CW:(kk + 1) * CW], lo(u)[:, kk * CW:(kk + 1) * CW],
                                              start=k == 0, stop=k == 7)
                            ins.then_inc(unit_used, 1)
                    if 1 <= b <= NB:
                        pe.wait_ge(hid_ready, NT * b)
                        if b >= 2:
                            pe.wait_ge(hidT_lo, b - 1)
                        for j in range(2):
                            for t in range(NT):
                                ins = m.transpose(ps[2][:, j * T + t * P:j * T + (t + 1) * P],
                                                  hid[:, (b - 1) % 2, t, j * P:(j + 1) * P], ident[:])
                        ins.then_inc(hid_turned, 1)
                    if b >= 2:
                        pe.wait_ge(hidT_lo, b - 1)
                        rows_out(U_FFN + down_pos[b - 2], lambda kk, t: hidTh[:, b % 2, kk, t * P:(t + 1) * P],
                                 lambda kk, t: hidTl[:, b % 2, kk, t * P:(t + 1) * P], 4, b == 2, b == NB + 1)
                    if b == NB - 2:
                        turn_embedding(0)

            dense_ffn()

            def ple(l, r, base_unit, nth):
                turn(r)
                for i in range(KD // 2):
                    pe.wait_ge(h_ready, (KD // 2) * (nth + 1))
                    rows_out(base_unit + 1 + i, lambda kk, t: hTh[:, 2 * i + kk, t * P:(t + 1) * P],
                             lambda kk, t: hTl[:, 2 * i + kk, t * P:(t + 1) * P], 4, i == 0, i == KD // 2 - 1)

            rows_out(U_PLE0, lambda kk, t: pTh[:, kk, t * P:(t + 1) * P], lambda kk, t: pTl[:, kk, t * P:(t + 1) * P],
                     0, True, True)
            ple(0, XR_PLE0, U_PLE0, 2)

            def mlstm():
                turn(XR_MLSTM)

                def project(i):
                    pe.wait_ge(bd_ready, i + 1)
                    pe.wait_ge(xc_ready, i + 1)
                    for pr in range(2):
                        n0 = (2 * i + pr) * 4
                        for j in range(4):
                            item = n0 + j
                            if item >= 3:
                                prev = item - 3
                                pq, pj = prev // 4, prev % 4
                                if pj < 2:
                                    pe.wait_ge(qk_copied, 2 * pq + pj + 1)
                                else:
                                    pe.wait_ge(v_copied, 2 * pq + pj - 1)
                            bank = ps[4 + item % 3]
                            for k in range(2):
                                cc = 2 * pr + k
                                if j < 2:
                                    ins = m.matmul(bank[:, k * T:(k + 1) * T], blockdiag[:, j, cc, :], xc(4 * i + cc)[:, 0, :], start=True, stop=True)
                                elif j == 2:
                                    ins = m.matmul(bank[:, k * T:(k + 1) * T], blockdiag[:, 2, cc, :], xpad[:, cc, CONV - 1:], start=True, stop=True)
                                else:
                                    for t in range(NT):
                                        ins = m.matmul(bank[:, t * 2 * P + k * P:t * 2 * P + (k + 1) * P],
                                                       xpad[:, cc, CONV - 1 + t * P:CONV - 1 + (t + 1) * P],
                                                       blockdiag[:, 2, cc, :], start=True, stop=True)
                            ins.then_inc(qkv_mm, 1)
                        pe.wait_ge(qk_copied, 2 * (2 * i + pr) + 2)
                        pe.wait_ge(v_copied, 2 * (2 * i + pr) + 1)
                        for k in range(2):
                            c = 4 * i + 2 * pr + k
                            for j, src in enumerate((qT[:, c, :], kT[:, c, :], vT[:, k, :])):
                                for t in range(NT):
                                    ins = m.matmul(ps[7][:, t * 2 * H:(t + 1) * 2 * H], src[:, t * P:(t + 1) * P],
                                                   w_gate[:, j * KI + c, :], start=c == 0 and j == 0 and t == 0, stop=False,
                                                   skip_group_check=True)
                        if pr == 1:
                            ins.then_inc(bd_used, 1)

                for i in range(4):
                    if i >= 2:
                        pe.wait_ge(xm_copied, i - 1)
                    for hf in range(2):
                        features_out(U_MIN + 2 * i, hf, (2 * (i % 2), 2 * (i % 2) + 1), 3, i == 0)
                    if i:
                        project(i - 1)

                def z_block(i, hf, cgs=range(4)):
                    if i == 1:
                        pe.wait_ge(xm_copied, 4)
                    if i >= 2:
                        pe.wait_ge(z_copied, 2 + 4 * (i - 2))
                    features_out(U_MIN + 8 + 2 * i, hf, (Z_BANKS[i], Z_BANKS[i] + 1), 3, False, cgs)

                pe.wait_ge(xm_copied, 3)
                for hf in range(2):
                    z_block(0, hf)
                project(3)
                for t in range(NT):
                    ins = m.matmul(ps[7][:, t * 2 * H:(t + 1) * 2 * H], ones[0:1, :], b_gate[0:1, :], start=False, stop=t == NT - 1,
                                   skip_group_check=True)
                ins.then_inc(gates_mm, 1)
                z_block(1, 0)
                pe.wait_ge(logf_ready, 1)
                m.matmul(ps[7][:, 64:64 + H], tri_incl[:], logf[:, 0, :], start=True, stop=True)
                m.matmul(ps[7][:, 64 + H:64 + 2 * H], ones[:], logf[:, 0, :], start=True, stop=False)
                m.matmul(ps[7][:, 64 + H:64 + 2 * H], tri_incl[:], logf[:, 1, :], start=False, stop=True).then_inc(cums_mm, 1)
                z_block(1, 1, range(0, 2))
                pe.wait_ge(a_ready, 1)
                for t in range(NT):
                    ins = m.transpose(ps[7][0:H, 256 + t * P:256 + (t + 1) * P], a_tok[:, t, :], ident[:])
                ins.then_inc(a_turned, 1)
                z_block(1, 1, range(2, 4))
                pe.wait_ge(m_ready, 1)
                for t in range(NT):
                    ins = m.transpose(ps[7][:, 96 + t * H:96 + (t + 1) * H], scan[0][:, P + t * P:P + (t + 1) * P], ident[0:H, 0:H])
                ins.then_inc(m_turned, 1)

                def scores(h):
                    if h >= 2:
                        pe.wait_ge(p_weights, h - 1)
                    if h == 0:
                        pe.wait_ge(v_copied, 16)
                        pe.wait_ge(qk_copied, 16)
                    if h == 1:
                        pe.wait_ge(m_tok_ready, 1)
                    sb = ps[4 + h % 2]
                    for k in range(2):
                        m.matmul(sb[:, 0:T], kT[:, 2 * h + k, 0:P], qT[:, 2 * h + k, :], start=k == 0, stop=k == 1)
                    for k in range(2):
                        m.matmul(sb[:, T:T + P], kT[:, 2 * h + k, P:T], qT[:, 2 * h + k, P:T], start=k == 0, stop=k == 1)
                    m.matmul(ps[6 + h % 2][:, 0:T], ident[0:H, h:h + 1].to_broadcast([H, P]), scan[0][:, P:],
                             start=True, stop=True).then_inc(scores_mm, 1)

                def values(h):
                    pe.wait_ge(p_weights, h + 1)
                    if h:
                        pe.wait_ge(num_copied, h)
                        pe.wait_ge(qn_copied, h)
                    else:
                        pe.wait_ge(z_copied, 4)
                    vh = v_m[:, :, h * DH:(h + 1) * DH]
                    pw = pT[:, h % 2, :]
                    for t, srcs in ((0, ((0, 0),)), (1, ((0, P), (1, 2 * P)))):
                        for n, (s, c0) in enumerate(srcs):
                            m.matmul(ps[2][:, t * DH:(t + 1) * DH], pw[:, c0:c0 + P], vh[:, s, :], start=n == 0, stop=n == len(srcs) - 1)
                    for t, srcs in ((0, ((0, 0),)), (1, ((0, P), (1, 2 * P)))):
                        for n, (s, c0) in enumerate(srcs):
                            ins = m.matmul(ps[3][:, t:t + 1], pw[:, c0:c0 + P], ones[:, 0:1], start=n == 0, stop=n == len(srcs) - 1)
                    ins.then_inc(num_mm, 1)

                def turn_hn(g):
                    pe.wait_ge(hn_ready, g + 1)
                    if g >= 4:
                        pe.wait_ge(mixed_lo, g - 3)
                    for k in range(2):
                        for t in range(NT):
                            ins = m.transpose(ps[4 + g % 4][:, k * T + t * P:k * T + (t + 1) * P], num[:, g, t, k * P:(k + 1) * P], ident[:])
                    ins.then_inc(hn_turned, 1)

                for h in range(H):
                    scores(h)
                    if h:
                        values(h - 1)
                    if h < 6:
                        z_block(2 + h // 4, h % 4 // 2, range(h % 2 * 2, h % 2 * 2 + 2))
                values(H - 1)
                for g in range(4):
                    turn_hn(g)
                z_block(3, 1)
                for g in range(H):
                    pe.wait_ge(mixed_lo, g + 1)
                    if g == 0:
                        pe.wait_ge(z_copied, 8)
                        pe.wait_ge(num_copied, H)
                        pe.wait_ge(qn_copied, H)
                    rows_out(U_MOUT + g, lambda kk, t: ohi[:, 2 * g + kk, t * P:(t + 1) * P],
                             lambda kk, t: olo[:, 2 * g + kk, t * P:(t + 1) * P], 0, g == 0, g == H - 1)
                    if 1 <= g < 5:
                        turn_hn(g + 3)

            mlstm()

            def experts():
                turn(XR_MOE)
                for k in range(KD):
                    pe.wait_ge((hT32_even, hT32_odd)[k // 2 % 2], k // 4 + 1)
                    for t in range(NT):
                        ins = m.matmul(ps[0][:, t * E:(t + 1) * E], hT32[:, k, t * P:(t + 1) * P], router[:, k, :],
                                       start=k == 0 and t == 0, stop=k == KD - 1, skip_group_check=True)
                ins.then_inc(logits_mm, 1)
                pe.wait_ge(chosen_ready, 1)
                m.matmul(ps[1][:, 0:E], tri_strict[:], chosen[:, 0, :], start=True, stop=True)
                m.matmul(ps[1][:, E:2 * E], ones[:], chosen[:, 0, :], start=True, stop=False)
                m.matmul(ps[1][:, E:2 * E], tri_strict[:], chosen[:, 1, :], start=False, stop=True)
                for t in range(NT):
                    ins = m.matmul(ps[1][:, 2 * E:3 * E], ones[:], chosen[:, t, :], start=t == 0, stop=t == NT - 1)
                ins.then_inc(slots_mm, 1)
                pe.wait_ge(hl_ready, NT)
                pe.wait_ge(comb_ready, 1)
                pe.wait_ge(over_known, 1)
                with pe.If(pe.value_load(over[0:1, 0:1], min_val=0, max_val=1) > 0):
                    with pe.Fori(0, E) as e:
                        pe.wait_ge(o_picked, e * 3 + 3)
                        for t in range(NT):
                            m.transpose(ps[2][:, t * P:(t + 1) * P], o_pick[:, t, :], ident[:])
                        for t in range(NT):
                            m.matmul(ps[2][:, T:T + 1], o_pick[:, t, :], comb[:, t, bass.ds(e, 1)], start=t == 0, stop=t == NT - 1)
                        for k in range(KD):
                            for t in range(NT):
                                ins = m.matmul(ps[6 + k // 4][:, (k % 4) * P:(k % 4 + 1) * P], xn[:, t, k * P:(k + 1) * P],
                                               o_pick[:, t, :], start=t == 0, stop=t == NT - 1)
                        ins.then_inc(o_gathered, 1)
                        with pe.Fori(0, NB) as b:
                            pe.wait_ge(o_copied, e * 4 + 4)
                            pe.wait_ge(o_landed, (e * NB + b) * 48 + 48)
                            for j, w in enumerate((o_gate, o_up)):
                                for k in range(KD):
                                    ins = m.matmul(ps[0][:, j * FB:(j + 1) * FB], o_xg[:, k, :], w[:, k, :], start=k == 0, stop=k == KD - 1)
                            ins.then_inc(o_gu_mm, 1)
                            pe.wait_ge(o_hid_ready, e * NB + b + 1)
                            for j in range(2):
                                ins = m.transpose(ps[2][:, j * P:(j + 1) * P], o_hid[:, j * P:(j + 1) * P], ident[:])
                            ins.then_inc(o_hid_turned, 1)
                            pe.wait_ge(o_hidT_ready, e * NB + b + 1)
                            for h in range(2):
                                for j in range(2):
                                    ins = m.matmul(ps[4 + h][:], o_hidT[:, j, :], o_down[:, j, h * CW:(h + 1) * CW], start=j == 0, stop=j == 1)
                            ins.then_inc(o_down_mm, 1)
                            pe.wait_ge(o_y_added, e * NB + b + 2)
                        pe.wait_ge(o_y_ready, e * (NB + 1) + (NB + 1))
                        for q in range(4):
                            t, h = q // 2, q % 2
                            if q >= 2:
                                pe.wait_ge(o_added, e * 4 + q - 1)
                            m.matmul(ps[6 + h][:], o_pickT[:, t, :], o_y[:, h * CW:(h + 1) * CW], start=True, stop=True).then_inc(o_back, 1)
                        pe.wait_ge(o_added, e * 4 + 4)
                    pe.wait_ge(o_added, 4 * E)

                def gather(e, o):
                    pe.wait_ge(e_pick, e * NT + (o * NT + NT))
                    for k in range(KD):
                        for t in range(NT):
                            m.matmul(ps[6 + k // 4][:, (k % 4) * P:(k % 4 + 1) * P], hh[:, t, k * P:(k + 1) * P], pick[:, t, :],
                                     start=t == 0, stop=False)
                            ins = m.matmul(ps[6 + k // 4][:, (k % 4) * P:(k % 4 + 1) * P], hl[:, t, k * P:(k + 1) * P], pick[:, t, :],
                                           start=False, stop=t == NT - 1)
                        if k % 4 == 3:
                            ins.then_inc(e_gathered, 1)

                def turn_pick(e, o):
                    for t in range(NT):
                        m.transpose(ps[3][:, t * P:(t + 1) * P], pick[:, t, :].bitcast(F32), ident[:])
                    for t in range(NT):
                        ins = m.matmul(ps[3][:, T:T + 1], pick[:, t, :].bitcast(F32), comb[:, t, bass.ds(e + o, 1)], start=t == 0, stop=t == NT - 1)
                    ins.then_inc(e_pickT_mm, 1)

                def back(e, t, b0=6):
                    if t == 0:
                        pe.wait_ge(e_y_lo, e * 2 + 2)
                        pe.wait_ge(e_pickT, e + 1)
                    elif b0 == 6:
                        pe.wait_ge(e_added, e * 4 + 2)
                    for h in range(2):
                        m.matmul(ps[b0 + h][:], pickT[:, t, :], yh[:, h * CW:(h + 1) * CW], start=True, stop=False)
                        m.matmul(ps[b0 + h][:], pickT[:, t, :], yl[:, h * CW:(h + 1) * CW], start=False, stop=True).then_inc(e_back, 1)

                def blocks(e, o, span, more):
                    def unit(j, half):
                        pe.wait_ge(lo_ready, e * (2 * FU) + (2 * (o * FU + U_MOE + j) + half + 1))
                        return whi[:, (U_MOE + j) % HIS, :], wlo[:, j % SLOTS, :]

                    for b in span:
                        if b < NB:
                            for hf in range(2):
                                for kk in range(4):
                                    if kk % 2 == 0:
                                        wh, wl = unit(gu_pos[b] + hf, kk // 2)
                                    k = 4 * hf + kk
                                    if b == 0 and k % 4 == 0:
                                        pe.wait_ge(e_xg_lo, e * 2 + (o * 2 + k // 4 + 1))
                                    ins = mm3(ps[b % 2][:], xgh[:, k, :], xgl[:, k, :], wh[:, kk * CW:(kk + 1) * CW],
                                              wl[:, kk * CW:(kk + 1) * CW], start=k == 0, stop=k == 7)
                                ins.then_inc(unit_used, 1)
                        if 1 <= b <= NB:
                            pe.wait_ge(e_hid, e * NB + (o * NB + b))
                            if b > 1:
                                pe.wait_ge(e_hidT_lo, e * NB + (o * NB + b - 1))
                            for j in range(2):
                                ins = m.transpose(ps[2][:, j * P:(j + 1) * P], hid[:, (b - 1) % 2, 0, j * P:(j + 1) * P], ident[:])
                            ins.then_inc(e_hid_turned, 1)
                        if b == SPLIT_AT - 1:
                            if o:
                                pe.wait_ge(e_added, e * 4 + 4)
                            turn_pick(e, o)
                        if o and b == 1:
                            back(e, 0)
                        if b >= 2:
                            pe.wait_ge(e_hidT_lo, e * NB + (o * NB + b - 1))
                            for kk in range(2):
                                wh, wl = unit(down_pos[b - 2], kk)
                                for h in range(2):
                                    w0 = kk * D + h * CW
                                    ins = mm3(ps[4 + h][:], hidTh[:, b % 2, kk, 0:P], hidTl[:, b % 2, kk, 0:P],
                                              wh[:, w0:w0 + CW], wl[:, w0:w0 + CW],
                                              start=b == 2 and kk == 0, stop=b == NB + 1 and kk == 1)
                            ins.then_inc(unit_used, 1)
                        if o and b == 2:
                            back(e, 1)
                        if b == GATHER_AT:
                            if more:
                                gather(e, o + 1)
                            else:
                                turn_embedding(1)

                gather(0, 0)
                blocks(0, 0, range(SPLIT_AT), True)
                with pe.Fori(0, E - 1) as e:
                    blocks(e, 0, range(SPLIT_AT, NB + 2), True)
                    blocks(e, 1, range(SPLIT_AT), True)
                pe.wait_ge(e_pickT_c, E)
                blocks(E - 1, 0, range(SPLIT_AT, NB + 2), False)
                rows_out(U_PLE1, lambda kk, t: pTh[:, kk, t * P:(t + 1) * P], lambda kk, t: pTl[:, kk, t * P:(t + 1) * P],
                         0, True, True)
                for t in range(NT):
                    back(E - 1, t, (6, 4)[t])

            experts()
            ple(1, XR_PLE1, U_PLE1, 4)


_INS = ["x", "p", "norm_mix", "norm_ffn", "norm_ple", "norm_final", "ga_w_in", "ga_ln_g", "ga_ln_b", "ga_w_s", "ga_b_s",
        "ga_w_out", "mb_w_in", "mb_conv_w", "mb_conv_b", "mb_wq", "mb_wk", "mb_wv", "mb_w_gate", "mb_b_gate", "mb_norm_g",
        "mb_skip", "mb_w_out", "fd_w_gate", "fd_w_up", "fd_w_down", "fe_router", "fe_w_gate", "fe_w_up", "fe_w_down",
        "ple_w_proj", "ple_w_gate"]


def kernel(**inputs):
    import numpy as np
    import concourse.bacc as bacc
    from concourse.bass_utils import run_bass_kernel_spmd

    nc = bacc.Bacc("TRN2", target_bir_lowering=False, num_devices=1)
    arrays = {f"in_{name}": np.ascontiguousarray(inputs[name]) for name in _INS}
    aps = {name: nc.dram_tensor(f"in_{name}", arrays[f"in_{name}"].shape, mybir.dt.from_np(arrays[f"in_{name}"].dtype),
                                kind="ExternalInput").ap() for name in _INS}
    shape = inputs["x"].shape
    out = nc.dram_tensor("out_0", shape, F32, kind="ExternalOutput").ap()
    build(nc, aps, out)
    r = run_bass_kernel_spmd(nc, [arrays], core_ids=[0])
    return r.results[0]["out_0"]
```
